# Optimizing a Trainium2 kernel written in Bass

```python
import jax, jax.numpy as jnp
from jax import lax
import numpy as np

D_MODEL = 1024
BATCH = 1
SEQ = 1024
DEPTH = 2

CHUNK = 64
N_A_LAYERS = DEPTH // 2
N_B_LAYERS = DEPTH - N_A_LAYERS
POOL_WINDOWS = (2, 4, 8, 16)
N_POOL_GROUPS = len(POOL_WINDOWS)
POOL_GROUP_DIM = D_MODEL // N_POOL_GROUPS
HEAD_DIM = 64
N_HEADS = D_MODEL // HEAD_DIM
N_KV_HEADS = 4
GROUP = N_HEADS // N_KV_HEADS
WINDOW = 128
WINDOW_CHUNKS = WINDOW // CHUNK
BAND = WINDOW_CHUNKS * CHUNK
N_BUCKETS = 32
MAX_DISTANCE = 128
D_FF = 4 * D_MODEL
EPS = 1e-6
NEG_INF = -1e30

kernel_name = "yoco_pool_swa_sink_hybrid"

def rms_norm(x, g):
    xf = x.astype(jnp.float32)
    y = xf * lax.rsqrt(jnp.mean(xf * xf, axis=-1, keepdims=True) + EPS)
    return (y * g.astype(jnp.float32)).astype(x.dtype)

def t5_buckets():
    q_pos = np.arange(CHUNK)[:, None]
    k_pos = np.arange(BAND)[None, :] - (WINDOW_CHUNKS - 1) * CHUNK
    n = -(k_pos - q_pos)
    half = N_BUCKETS // 2
    ret = (n < 0).astype(np.int32) * half
    n = np.abs(n)
    max_exact = half // 2
    large = max_exact + (np.log(np.maximum(n, 1) / max_exact)
                         / np.log(MAX_DISTANCE / max_exact) * (half - max_exact)).astype(np.int32)
    large = np.minimum(large, half - 1)
    ret = ret + np.where(n < max_exact, n, large)
    return ret.astype(np.int32)

def band_valid(n_chunks):
    c = np.arange(n_chunks)[:, None]
    key_chunk = c - (WINDOW_CHUNKS - 1) + np.arange(BAND)[None, :] // CHUNK
    return key_chunk >= 0

def to_band(t):
    n_chunks = t.shape[1]
    tp = jnp.pad(t, ((0, 0), (WINDOW_CHUNKS - 1, 0), (0, 0), (0, 0), (0, 0)))
    return jnp.concatenate([tp[:, i:i + n_chunks] for i in range(WINDOW_CHUNKS)], axis=2)

def pool_mixer(xn, w, scale):
    B, S, _ = xn.shape
    xg = xn.astype(jnp.float32).reshape(B, S, N_POOL_GROUPS, POOL_GROUP_DIM)
    cs = jnp.cumsum(xg, axis=1)
    pos = jnp.arange(1, S + 1, dtype=jnp.float32)
    means = []
    for g, win in enumerate(POOL_WINDOWS):
        c = cs[:, :, g]
        lag = jnp.pad(c, ((0, 0), (win, 0), (0, 0)))[:, :S]
        cnt = jnp.minimum(pos, float(win))
        means.append((c - lag) / cnt[None, :, None])
    diff = (jnp.stack(means, axis=2) - xg).astype(xn.dtype)
    y = jnp.einsum('bsgc,gcd->bsgd', diff, w)
    return y.reshape(B, S, D_MODEL) * scale

def shared_kv(h, norm_kv_g, w_kv, b_kv):
    B, S, _ = h.shape
    kv = rms_norm(h, norm_kv_g) @ w_kv + b_kv
    k, v = jnp.split(kv, 2, axis=-1)
    shp = (B, S // CHUNK, CHUNK, N_KV_HEADS, HEAD_DIM)
    return to_band(k.reshape(shp)), to_band(v.reshape(shp))

def window_attention(xn, k_band, v_band, w_q, b_q, sinks, w_o, b_o, rel_bias):
    B, S, _ = xn.shape
    n_chunks = S // CHUNK
    q = (xn @ w_q + b_q).reshape(B, n_chunks, CHUNK, N_KV_HEADS, GROUP, HEAD_DIM)
    s = jnp.einsum('bnqkgd,bnjkd->bnkgqj', q.astype(jnp.float32),
                   k_band.astype(jnp.float32)) * (HEAD_DIM ** -0.5)
    bias = rel_bias.astype(jnp.float32)[t5_buckets()]
    bias = jnp.transpose(bias, (2, 0, 1)).reshape(N_KV_HEADS, GROUP, CHUNK, BAND)
    valid = jnp.asarray(band_valid(n_chunks))[None, :, None, None, None, :]
    s = jnp.where(valid, s + bias, NEG_INF)
    sink = sinks.astype(jnp.float32).reshape(N_KV_HEADS, GROUP)[None, None, :, :, None, None]
    m = jnp.maximum(jnp.max(s, axis=-1, keepdims=True), sink)
    p = jnp.exp(s - m)
    p = p / (jnp.sum(p, axis=-1, keepdims=True) + jnp.exp(sink - m))
    o = jnp.einsum('bnkgqj,bnjkd->bnqkgd', p.astype(v_band.dtype), v_band)
    return o.reshape(B, S, N_HEADS * HEAD_DIM) @ w_o + b_o

def sq_relu_mlp(xn, w_up, w_down):
    u = jax.nn.relu(xn @ w_up)
    return (u * u) @ w_down

def setup_inputs(seed: int = 0) -> dict:
    key = jax.random.key(seed)
    ks = jax.random.split(key, 17)
    f32 = jnp.float32
    nrm = lambda k, shp, sc: jax.random.normal(k, shp, f32) * sc
    qd = N_HEADS * HEAD_DIM
    kvd = 2 * N_KV_HEADS * HEAD_DIM
    return {
        "x": nrm(ks[0], (BATCH, SEQ, D_MODEL), 1.0),
        "norm_mix_g": 1.0 + nrm(ks[1], (DEPTH, D_MODEL), 0.02),
        "norm_mlp_g": 1.0 + nrm(ks[2], (DEPTH, D_MODEL), 0.02),
        "pool_w": nrm(ks[3], (N_A_LAYERS, N_POOL_GROUPS, POOL_GROUP_DIM, POOL_GROUP_DIM), POOL_GROUP_DIM ** -0.5),
        "pool_scale": 1.0 + nrm(ks[4], (N_A_LAYERS, D_MODEL), 0.02),
        "norm_kv_g": 1.0 + nrm(ks[5], (D_MODEL,), 0.02),
        "w_kv": nrm(ks[6], (D_MODEL, kvd), D_MODEL ** -0.5),
        "b_kv": nrm(ks[7], (kvd,), 0.02),
        "w_q": nrm(ks[8], (N_B_LAYERS, D_MODEL, qd), D_MODEL ** -0.5),
        "b_q": nrm(ks[9], (N_B_LAYERS, qd), 0.02),
        "sinks": nrm(ks[10], (N_B_LAYERS, N_HEADS), 1.0),
        "rel_bias": nrm(ks[11], (N_BUCKETS, N_HEADS), 0.5),
        "w_o": nrm(ks[12], (N_B_LAYERS, qd, D_MODEL), qd ** -0.5),
        "b_o": nrm(ks[13], (N_B_LAYERS, D_MODEL), 0.02),
        "w_up": nrm(ks[14], (DEPTH, D_MODEL, D_FF), D_MODEL ** -0.5),
        "w_down": nrm(ks[15], (DEPTH, D_FF, D_MODEL), D_FF ** -0.5),
        "norm_f_g": 1.0 + nrm(ks[16], (D_MODEL,), 0.02),
    }

def reference(x, norm_mix_g, norm_mlp_g, pool_w, pool_scale, norm_kv_g, w_kv, b_kv,
              w_q, b_q, sinks, rel_bias, w_o, b_o, w_up, w_down, norm_f_g):
    h = x
    k_band = v_band = None
    for l in range(DEPTH):
        if l == N_A_LAYERS:
            k_band, v_band = shared_kv(h, norm_kv_g, w_kv, b_kv)
        hn = rms_norm(h, norm_mix_g[l])
        if l < N_A_LAYERS:
            h = h + pool_mixer(hn, pool_w[l], pool_scale[l])
        else:
            j = l - N_A_LAYERS
            h = h + window_attention(hn, k_band, v_band, w_q[j], b_q[j], sinks[j],
                                     w_o[j], b_o[j], rel_bias)
        h = h + sq_relu_mlp(rms_norm(h, norm_mlp_g[l]), w_up[l], w_down[l])
    return rms_norm(h, norm_f_g)


_drawn_inputs = setup_inputs


def setup_inputs(seed=0):
    import zlib

    import numpy as np

    out = dict(_drawn_inputs(seed))
    spreads = {}
    factors = {'norm_mix_g': 3.763,
     'pool_scale': 3.856,
     'norm_kv_g': 26.237,
     'b_kv': 116.383,
     'b_q': 8.0,
     'sinks': 64.0,
     'b_o': 112.192,
     'norm_f_g': 23.167,
     'norm_mlp_g': 5.879,
     'rel_bias': 3.649}
    for name, (base, spread) in spreads.items():
        noise = np.random.default_rng([zlib.crc32(name.encode()), seed]).standard_normal(out[name].shape)
        drawn = base * np.exp(spread * noise) if base else spread * noise
        out[name] = __import__('jax').numpy.asarray(drawn.astype(out[name].dtype))
    for name, factor in factors.items():
        out[name] = (out[name] * factor).astype(out[name].dtype)
    return out
```

```python
from contextlib import ExitStack

import concourse.bass as bass
import numpy as np
from concourse import mybir

F32 = mybir.dt.float32
F32R = mybir.dt.float32r
ALU = mybir.AluOpType
ACT = mybir.ActivationFunctionType
AX = mybir.AxisListType

P = 128
SEQ, D, D_FF = 1024, 1024, 4096
NT = SEQ // P
HALF = SEQ // 2
HT = HALF // P
DC = D // P
CHUNK, HEAD_DIM, N_HEADS, N_KV, GROUP = 64, 64, 16, 4, 4
BAND = 2 * CHUNK
KV_D = N_KV * HEAD_DIM
WINDOWS = (2, 4, 8, 16)
GROUP_DIM = D // len(WINDOWS)
N_BUCKETS, MAX_DISTANCE = 32, 128
N_DIAG = 192
EPS = 1e-6
NEG_INF = -1e30
FB = 256
NB = D_FF // FB
QUAD, PIECE = 2048, 1024

POOL_Q = 0
UP_Q = (1, 51)
KV_Q = 33
Q_Q = (35, 39)
O_Q = (43, 47)

UP_SLOT, DOWN_SLOT = 1, 0

POOLING, MLP0, ATTN, MLP1, FINAL = range(5)

STEPS = 16


def t5_diagonals():
    n = 127 - np.arange(N_DIAG - 1)
    half = N_BUCKETS // 2
    ret = (n < 0).astype(np.int32) * half
    n = np.abs(n)
    max_exact = half // 2
    large = max_exact + (np.log(np.maximum(n, 1) / max_exact)
                         / np.log(MAX_DISTANCE / max_exact) * (half - max_exact)).astype(np.int32)
    ret = ret + np.where(n < max_exact, n, np.minimum(large, half - 1))
    one_hot = np.zeros((N_BUCKETS, N_DIAG), np.float32)
    one_hot[ret, np.arange(N_DIAG - 1)] = 1.0
    return one_hot


def pool_bands():
    band = np.zeros((P, len(WINDOWS), 3, P), np.float32)
    t = np.arange(P)
    for g, w in enumerate(WINDOWS):
        lag = t[None, :] - t[:, None]
        inside = (lag >= 0) & (lag < w)
        band[:, g, 0] = inside / np.float32(w) - (lag == 0)
        band[:, g, 1] = inside / np.minimum(t + 1, w).astype(np.float32)[None, :] - (lag == 0)
        band[:, g, 2] = (lag + P < w) / np.float32(w)
    return band


def at_least(eng, sem, value):
    if not (isinstance(value, int) and value <= 0):
        eng.wait_ge(sem, value)


def trunk(nc, x, mix_g, mlp_g, kv_g, pool_w, pool_scale, w_kv, b_k, b_v, w_q, b_q, sinks, rel_bias,
          w_o, b_o, w_up, w_down, norm_f_g, bands_in, one_hot_in, ident_in, out):
    ctx = ExitStack()
    with ctx:
        def sb(name, shape, dt=F32):
            return ctx.enter_context(nc.sbuf_tensor(name, shape, dt))

        def sem(name):
            return ctx.enter_context(nc.semaphore(name))

        h = sb("h", [P, NT, D])
        acts = [sb(f"acts{i}", [P, 2, DC, HALF], F32R) for i in range(2)]
        normed = sb("normed", [P, HT, D])
        wring = sb("wring", [P, 2, 2, QUAD], F32R)
        wraw = sb("wraw", [P, 2, PIECE])
        tmp = sb("tmp", [P, 4, 512])
        ident = sb("ident", [P, P])
        gains = sb("gains", [P, 5, DC])
        bq_col = sb("bq_col", [P, DC])
        bk_col = sb("bk_col", [P, 2])
        bv_row = sb("bv_row", [P, KV_D])
        sink = sb("sink", [P, DC])
        neg_sink = sb("neg_sink", [P, DC])
        neg_half = sb("neg_half", [P, 1])
        sumsq = sb("sumsq", [P, NT])
        variance = sb("variance", [P, NT])
        rstd = sb("rstd", [P, NT])
        neg_max = sb("neg_max", [P, 2, 4])
        sink_gap = sb("sink_gap", [P, 2, 4])
        psum_row = sb("psum_row", [P, 2, 4])
        sink_exp = sb("sink_exp", [P, 2, 4])
        denom = sb("denom", [P, 2, 4])
        inv_denom = sb("inv_denom", [P, 2, 4])

        with nc.sbuf_tensor("squares", [P, 2, 2, 2, 512], F32R) as squares:
            pass
        q1 = sb("q1", [P, 2, HALF // CHUNK, GROUP, CHUNK])
        with ExitStack() as early:
            def sb_early(name, shape):
                return early.enter_context(nc.sbuf_tensor(name, shape, F32))
            bands = sb_early("bands", [P, len(WINDOWS), 3, P])
            scale_row = sb_early("scale_row", [P, D])
            before = sb_early("before", [P, D])
            diag = sb_early("diag", [N_HEADS, N_DIAG])
            one_hot = sb_early("one_hot", [N_BUCKETS, N_DIAG])
            rel = sb_early("rel", [N_BUCKETS, N_HEADS])
        with nc.sbuf_tensor("gf_row", [P, D], F32) as gf_row:
            pass
        kT = sb("kT", [P, 2, CHUNK + SEQ])
        v = sb("v", [P, NT, KV_D])
        v_shift = sb("v_shift", [P, NT, KV_D])
        bias = sb("bias", [P, N_HEADS // 2, BAND])

        queries = [normed[:, :, :].rearrange("p a b -> p (a b)").rearrange(
            "p (i n g t) -> p i n g t", i=2, g=GROUP, t=CHUNK), q1[:, :, :, :, :]]
        relu, sq = tmp[:, 0:2, :], tmp[:, 2:4, :]
        probs, probsT = tmp[:, 0:2, :], tmp[:, 2:4, :]
        junk = tmp[:, 0:2, :].rearrange("p a b -> p (a b)")
        bo_row = tmp[:, 2:4, :].rearrange("p a b -> p (a b)")

        banks = ctx.enter_context(nc.psum_tensor("banks", [P, 8, 512], F32))
        bank = [banks[:, i, :] for i in range(8)]
        U = bank[0:2]
        DN = bank[2:6]
        T = bank[6:8]
        PT, PV = bank[4], bank[5]

        diag_dram = nc.dram_tensor("diag_dram", [N_HEADS, CHUNK, N_DIAG], F32, kind="Internal").ap()

        x_in = [sem(f"x_in{t}") for t in range(NT)]
        consts_in = sem("consts_in")
        early_in = sem("early_in")
        raw_in = [sem(f"raw_in{i}") for i in range(2)]
        w_hi, w_lo = sem("w_hi"), sem("w_lo")
        w_scaled = sem("w_scaled")
        ss_done, var_done, rstd_done = sem("ss_done"), sem("var_done"), sem("rstd_done")
        half_set = sem("half_set")
        normed_done, before_done = sem("normed_done"), sem("before_done")
        t_full, t_hi, t_lo = sem("t_full"), sem("t_hi"), sem("t_lo")
        pool_full, pool_added = sem("pool_full"), sem("pool_added")
        diag_full, diag_copied, diag_out, bias_in = sem("diag_full"), sem("diag_copied"), sem("diag_out"), sem("bias_in")
        up_full, up_relu, up_sq, up_hi, up_lo = (sem(n) for n in ("up_full", "up_relu", "up_sq", "up_hi", "up_lo"))
        down_full, down_added = sem("down_full"), sem("down_added")
        kq_full, kq_out = sem("kq_full"), sem("kq_out")
        vo_full, vo_out = sem("vo_full"), sem("vo_out")
        shifted, pad_set = [sem(f"shifted{i}") for i in range(2)], sem("pad_set")
        bo_in, bo_added = sem("bo_in"), sem("bo_added")
        sink_neg = sem("sink_neg")
        s_full, logits_done, exp_done, probs_done = (
            sem(n) for n in ("s_full", "logits_done", "exp_done", "probs_done"))
        pt_full, pt_copied, pv_full, o_hi, o_lo = (
            sem(n) for n in ("pt_full", "pt_copied", "pv_full", "o_hi", "o_lo"))
        dve_step = sem("dve_step")
        gf_in, final_done = sem("gf_in"), sem("final_done")
        out_done = [sem(f"out_done{t}") for t in range(NT)]

        def quad(j, part, n):
            return wring[:, j % 2, part, :].rearrange("p (c n) -> p c n", n=n)

        def kv_part(part, c):
            return quad(KV_Q + c // 4, part, 512)[:, c % 4, :]

        def score_banks(a):
            return 6 if a % 2 == 0 else 2 if a < STEPS else 0

        def o_count(half, i, tt):
            return NT + 16 * half + 4 * i + tt

        block = ctx.enter_context(nc.Block())

        @block.sync
        def _(sp):
            x_tiles = x.rearrange("(t p) d -> t p d", p=P)
            out_tiles = out.rearrange("(t p) d -> t p d", p=P)
            pool_v = pool_w.rearrange("g (k p) d -> p g k d", p=P)
            kv_v = w_kv.rearrange("(c p) n -> p c n", p=P)
            q_v = w_q.rearrange("(c p) n -> p c n", p=P)
            o_v = w_o.rearrange("(c p) n -> p c n", p=P)
            up_v = [w_up[i].rearrange("(c p) n -> p c n", p=P) for i in range(2)]

            def load(j, e, source, n):
                at_least(sp, w_lo, 2 * j + e - 1)
                dst = wraw[:, e, :].rearrange("p (c n) -> p c n", n=n)
                sp.dma_start(dst, source).then_inc(raw_in[e], 16)

            def load_mlp(layer, b):
                for e in range(2):
                    load(UP_Q[layer] + 2 * b, e, up_v[layer][:, 4 * e:4 * e + 4, bass.ds(b * FB, FB)], FB)
                for e in range(2):
                    load(UP_Q[layer] + 2 * b + 1, e,
                         w_down[layer][bass.ds(b * FB + e * P, P), :].rearrange("p (c n) -> p c n", c=1), D)

            for t in range(HT):
                sp.dma_start(h[:, t, :], x_tiles[t]).then_inc(x_in[t], 16)
            for e in range(2):
                load(POOL_Q, e, pool_v[:, 2 * e:2 * e + 2].rearrange("p g k d -> p (g k) d"), GROUP_DIM)
            for t in range(HT, NT):
                sp.dma_start(h[:, t, :], x_tiles[t]).then_inc(x_in[t], 16)

            with sp.Fori(0, NB) as b:
                load_mlp(0, b)
            for c in range(2):
                for e in range(2):
                    load(KV_Q + c, e, kv_v[:, 4 * c + 2 * e:4 * c + 2 * e + 2, :], 512)
            for base, view in ((Q_Q[0], q_v), (Q_Q[1], q_v), (O_Q[0], o_v), (O_Q[1], o_v)):
                for i in range(4):
                    for e in range(2):
                        load(base + i, e, view[:, 4 * e:4 * e + 4, i * FB:(i + 1) * FB], FB)
            with sp.Fori(0, NB) as b:
                load_mlp(1, b)

            for t in range(NT):
                sp.wait_ge(final_done, t + 1)
                sp.dma_start(out_tiles[t], normed[:, t % HT, :]).then_inc(out_done[t], 16)
            for t in range(NT):
                sp.wait_ge(out_done[t], 16)

        @block.gpsimd
        def _(pool):
            pool.memset(neg_half[:, :], -0.5).then_inc(half_set, 1)
            early_loads = [
                (bands[:, :, :, :], bands_in), (scale_row[:, :], pool_scale.partition_broadcast(P)),
                (one_hot[:, :], one_hot_in), (rel[:, :], rel_bias),
            ]
            for dst, src in early_loads:
                pool.dma_start(dst, src).then_inc(early_in, 16)
            pool.wait_ge(half_set, 1)

            def rstd_of(stage, tiles):
                for t in tiles:
                    n = NT * stage + t
                    pool.wait_ge(ss_done, n + 1)
                    at_least(pool, normed_done, n + 1 - NT)
                    pool.tensor_scalar(variance[:, t:t + 1], sumsq[:, t:t + 1], 1.0 / D, EPS,
                                       ALU.mult, ALU.add).then_inc(var_done, 1)
                    pool.wait_ge(var_done, n + 1)
                    pool.tensor_tensor(rstd[:, t:t + 1], variance[:, t:t + 1], neg_half[:, :],
                                       ALU.pow).then_inc(rstd_done, 1)

            half_tiles = [range(0, HT), range(HT, NT)]
            rstd_of(POOLING, half_tiles[0])
            pool.wait_ge(diag_copied, 1)
            pool.dma_start(diag_dram, diag[:, :].rearrange("h (a n) -> h a n", a=1).to_broadcast(
                [N_HEADS, CHUNK, N_DIAG])).then_inc(diag_out, 16)
            rstd_of(POOLING, half_tiles[1])
            rstd_of(MLP0, half_tiles[0])
            rstd_of(MLP0, half_tiles[1])

            pool.wait_ge(pool_added, 2 * NT)
            pool.wait_ge(w_scaled, 2)
            pool.wait_ge(diag_out, 16)
            pool.memset(kT[:, :, 0:CHUNK], 0.0).then_inc(pad_set, 1)
            pool.memset(v_shift[0:CHUNK, 0, :], 0.0).then_inc(pad_set, 1)
            for i in range(2):
                rows = bass.AP(diag_dram.tensor, i * CHUNK * N_DIAG + CHUNK - 1,
                               [[N_DIAG - 1, CHUNK], [2 * CHUNK * N_DIAG, N_HEADS // 2], [1, BAND]])
                pool.dma_start(bias[CHUNK * i:CHUNK * i + CHUNK, :, :], rows).then_inc(bias_in, 16)
            pool.wait_ge(up_lo, 4 * NB)
            pool.wait_ge(up_hi, 4 * NB)
            pool.dma_start(bo_row, b_o.partition_broadcast(P)).then_inc(bo_in, 16)

            def add_bo(tiles):
                pool.wait_ge(bo_in, 16)
                for t in tiles:
                    pool.wait_ge(normed_done, NT * ATTN + t + 1)
                    pool.tensor_tensor(h[:, t, :], h[:, t, :], bo_row, ALU.add).then_inc(bo_added, 1)

            def shift_values(half):
                for t in half_tiles[half]:
                    pool.wait_ge(vo_out, t + 1)
                    pool.dma_start(v_shift[CHUNK:P, t, :], v[0:CHUNK, t, :]).then_inc(shifted[half], 16)
                    if t + 1 < NT:
                        pool.dma_start(v_shift[0:CHUNK, t + 1, :], v[CHUNK:P, t, :]).then_inc(shifted[half], 16)

            rstd_of(ATTN, half_tiles[0])
            add_bo(half_tiles[0])
            rstd_of(ATTN, half_tiles[1])
            add_bo(half_tiles[1])
            shift_values(0)
            shift_values(1)
            rstd_of(MLP1, half_tiles[0])
            rstd_of(MLP1, half_tiles[1])
            pool.wait_ge(pv_full, SEQ // CHUNK)
            pool.dma_start(gf_row[:, :], norm_f_g.partition_broadcast(P)).then_inc(gf_in, 16)
            rstd_of(FINAL, half_tiles[0])
            rstd_of(FINAL, half_tiles[1])

        @block.scalar
        def _(act):
            for dst, src in ((ident[:, :], ident_in), (gains[:, 0:2, :], mix_g), (gains[:, 2:4, :], mlp_g),
                             (gains[:, 4, :], kv_g), (bq_col[:, :], b_q), (bk_col[:, :], b_k),
                             (bv_row[:, :], b_v.partition_broadcast(P)),
                             (sink[0:CHUNK, :], sinks[0].partition_broadcast(CHUNK)),
                             (sink[CHUNK:P, :], sinks[1].partition_broadcast(CHUNK))):
                act.dma_start(dst, src).then_inc(consts_in, 16)

            def sum_squares(stage, half):
                for t in range(HT * half, HT * half + HT):
                    n = NT * stage + t
                    if stage == POOLING:
                        act.wait_ge(x_in[t], 16)
                    elif stage == MLP0:
                        act.wait_ge(pool_added, 2 * t + 2)
                    elif stage == ATTN or stage == FINAL:
                        layer = 0 if stage == ATTN else 1
                        act.wait_ge(down_added, 16 * NB * (layer + 1) - 2 * (NT - t) + 2)
                    else:
                        act.wait_ge(vo_out, o_count(half, 3, t % HT) + 1)
                    at_least(act, rstd_done, n + 1 - NT)
                    at_least(act, ss_done, n)
                    act.activation(junk, h[:, t, :], ACT.Square,
                                   accum_out=sumsq[:, t:t + 1]).then_inc(ss_done, 1)

            def transposed_hi(stage, half, gain):
                for c in range(DC):
                    n = 16 * stage + 8 * half + c
                    act.wait_ge(t_full, n + 1)
                    scale = 1.0 if gain is None else gains[:, gain, c:c + 1]
                    act.activation(acts[half][:, 0, c, :], T[n % 2][:, :], ACT.Copy,
                                   scale=scale).then_inc(t_hi, 1)

            def projection_used(j):
                for half in range(2):
                    if Q_Q[half] <= j < Q_Q[half] + 4:
                        act.wait_ge(kq_full, 4 + 8 * half + 2 * (j - Q_Q[half]) + 2)
                    if O_Q[half] <= j < O_Q[half] + 4:
                        act.wait_ge(vo_full, o_count(half, j - O_Q[half], HT - 1) + 1)

            def split_hi(j, gain=None, n=QUAD, slot=None, pooling=False):
                slot = j % 2 if slot is None else slot
                for e in range(2):
                    if pooling:
                        act.wait_ge(w_scaled, e + 1)
                    else:
                        at_least(act, raw_in[e], 16 * (j + 1))
                    if gain is None:
                        act.activation(wring[:, slot, 0, e * PIECE:(e + 1) * PIECE], wraw[:, e, :],
                                       ACT.Copy).then_inc(w_hi, 1)
                        continue
                    per = PIECE // n
                    for i in range(per):
                        c = (2 * ((j - KV_Q) * 2 + e) if n == 512 else 4 * e) + i
                        last = act.activation(quad(j, 0, n)[:, per * e + i, :], wraw[:, e, i * n:(i + 1) * n],
                                              ACT.Copy, scale=gains[:, gain, c:c + 1])
                    last.then_inc(w_hi, 1)

            def up_tile(layer, b, half, f):
                n = 4 * (NB * layer + b) + 2 * half + f
                act.wait_ge(up_full, n + 1)
                at_least(act, up_sq, n - 1)
                act.activation(relu[:, f, :], U[f][:, :], ACT.Relu).then_inc(up_relu, 1)
                act.wait_ge(up_sq, n + 1)
                at_least(act, down_full, 16 * (NB * layer + b) + 8 * half - 8)
                act.activation(squares[:, half, 0, f, :], sq[:, f, :], ACT.Copy).then_inc(up_hi, 1)

            def mlp_block(layer, b, before_down=None, after_first_half=None, next_up=True):
                if before_down:
                    before_down()
                else:
                    act.wait_ge(down_full, 16 * (NB * layer + b))
                split_hi(UP_Q[layer] + 2 * b + 1, slot=DOWN_SLOT)
                for f in range(2):
                    up_tile(layer, b, 0, f)
                if after_first_half:
                    after_first_half()
                for f in range(2):
                    up_tile(layer, b, 1, f)
                if next_up:
                    act.wait_ge(up_full, 4 * (NB * layer + b) + 4)
                    split_hi(UP_Q[layer] + 2 * b + 2, slot=UP_SLOT)

            def mlp(layer, stage, gain):
                def second_half():
                    transposed_hi(stage, 1, gain)
                act.wait_ge(ss_done, NT * (stage + 1))
                def down_slot_used():
                    if layer == 0:
                        act.wait_ge(pool_full, 2 * NT)
                    else:
                        projection_used(O_Q[1] + 3)
                mlp_block(layer, 0, down_slot_used, second_half)
                with act.Fori(1, NB - 1) as b:
                    mlp_block(layer, b)
                mlp_block(layer, NB - 1, next_up=False)

            sum_squares(POOLING, 0)
            act.wait_ge(diag_full, 1)
            act.activation(diag[:, :], DN[0][0:N_HEADS, 0:N_DIAG], ACT.Copy).then_inc(diag_copied, 1)
            sum_squares(POOLING, 1)
            act.wait_ge(consts_in, 16 * 9)
            transposed_hi(POOLING, 0, 0)
            split_hi(POOL_Q, pooling=True)
            transposed_hi(POOLING, 1, 0)
            sum_squares(MLP0, 0)
            split_hi(UP_Q[0])
            transposed_hi(MLP0, 0, 2)
            sum_squares(MLP0, 1)
            mlp(0, MLP0, 2)

            act.wait_ge(up_full, 4 * NB)
            split_hi(KV_Q, 4, 512)
            sum_squares(ATTN, 0)
            transposed_hi(ATTN, 0, None)
            act.wait_ge(down_full, 16 * NB)
            split_hi(KV_Q + 1, 4, 512)
            sum_squares(ATTN, 1)
            act.activation(neg_sink[:, :], sink[:, :], ACT.Copy, scale=-1.0).then_inc(sink_neg, 1)

            def key_out(half, i):
                act.wait_ge(kq_full, 2 * half + i + 1)
                act.activation(kT[:, i, CHUNK + HALF * half:CHUNK + HALF * half + HALF], U[i][:, :],
                               ACT.Identity, bias=bk_col[:, i:i + 1]).then_inc(kq_out, 1)

            def query_out(half, tile):
                n = 4 + 8 * half + tile
                act.wait_ge(kq_full, n + 1)
                act.activation(queries[half][:, tile // GROUP, :, tile % GROUP, :],
                               U[n % 2][:, :].rearrange("p (n t) -> p n t", t=CHUNK),
                               ACT.Identity, bias=bq_col[:, tile:tile + 1]).then_inc(kq_out, 1)

            act.wait_ge(pool_added, 2 * NT)
            act.wait_ge(diag_out, 16)
            key_out(0, 0)
            key_out(0, 1)
            transposed_hi(ATTN, 1, None)
            key_out(1, 0)
            key_out(1, 1)
            act.wait_ge(vo_full, NT)
            split_hi(Q_Q[0], 1, FB)
            split_hi(Q_Q[0] + 1, 1, FB)
            act.wait_ge(t_full, 16 * MLP1)
            for i in range(4):
                query_out(0, 2 * i)
                query_out(0, 2 * i + 1)
                projection_used(Q_Q[0] + i)
                split_hi(Q_Q[0] + 2 + i, 1, FB)

            def exponentials(a):
                act.wait_ge(logits_done, a + 1)
                for s in range(4):
                    act.activation(probs[:, a % 2, s * P:(s + 1) * P], probs[:, a % 2, s * P:(s + 1) * P],
                                   ACT.Exp, bias=neg_max[:, a % 2, s:s + 1],
                                   accum_out=psum_row[:, a % 2, s:s + 1])
                act.activation(sink_exp[:, a % 2, :], sink_gap[:, a % 2, :], ACT.Exp).then_inc(exp_done, 1)

            exponentials(0)
            act.wait_ge(bo_added, NT)
            for a in range(2 * STEPS):
                half, step = a // STEPS, a % STEPS
                if a + 1 < 2 * STEPS:
                    exponentials(a + 1)
                if half == 0 and a % 2:
                    query_out(1, a // 2)
                act.wait_ge(pt_full, a + 1)
                at_least(act, pv_full, (a - 2) // 2 + 1 if a % 2 else (a - 2) // 2)
                act.activation(probsT[:, a % 2, :], PT[:, :], ACT.Copy).then_inc(pt_copied, 1)
                if a % 2:
                    n = a // 2
                    act.wait_ge(pv_full, n + 1)
                    act.activation(acts[half][:, 0, :, CHUNK * (n % 8):CHUNK * (n % 8) + CHUNK],
                                   PV[:, :].rearrange("p (c t) -> p c t", t=CHUNK), ACT.Copy).then_inc(o_hi, 1)
                if a % 4 == 3:
                    j = Q_Q[1] + a // 4 + 2
                    projection_used(j - 2)
                    if j < O_Q[0]:
                        split_hi(j, 1, FB)
                    else:
                        split_hi(j)
            sum_squares(MLP1, 0)
            for i in range(2):
                projection_used(O_Q[1] + i)
                split_hi(O_Q[1] + 2 + i)
            transposed_hi(MLP1, 0, 3)
            projection_used(O_Q[1] + 2)
            split_hi(UP_Q[1])
            sum_squares(MLP1, 1)
            mlp(1, MLP1, 3)
            sum_squares(FINAL, 0)
            sum_squares(FINAL, 1)

        @block.tensor
        def _(pe):
            def three_passes(dst, terms, start=True, stop=True):
                last_term = len(terms) - 1
                for i, (lhsT, rhs) in enumerate(terms):
                    pe.matmul(dst, lhsT(0), rhs(0), start=start and i == 0, stop=False)
                    pe.matmul(dst, lhsT(0), rhs(1), start=False, stop=False)
                    mm = pe.matmul(dst, lhsT(1), rhs(0), start=False, stop=stop and i == last_term)
                return mm

            def transposes(stage, half):
                for c in range(DC):
                    n = 16 * stage + 8 * half + c
                    if c == 0:
                        pe.wait_ge(normed_done, NT * stage + HT * (half + 1))
                    at_least(pe, t_lo, n - 1)
                    for t in range(HT):
                        mm = pe.transpose(T[n % 2][:, t * P:(t + 1) * P], normed[:, t, c * P:(c + 1) * P],
                                          ident[:, :])
                    mm.then_inc(t_full, 1)

            def pool_differences(half):
                pe.wait_ge(normed_done, HT * (half + 1))
                if half:
                    pe.wait_ge(before_done, 1)
                for c in range(DC):
                    n = 8 * half + c
                    at_least(pe, t_lo, n - 1)
                    w = c * P // GROUP_DIM
                    cols = slice(c * P, (c + 1) * P)
                    for t in range(HT):
                        first = half == 0 and t == 0
                        mm = pe.matmul(T[n % 2][:, t * P:(t + 1) * P], normed[:, t, cols],
                                       bands[:, w, int(first), :], start=True, stop=first)
                        if not first:
                            prev = before[96:P, cols] if t == 0 else normed[96:P, t - 1, cols]
                            mm = pe.matmul(T[n % 2][:, t * P:t * P + 16], prev, bands[96:P, w, 2, 0:16],
                                           start=False, stop=True)
                    mm.then_inc(t_full, 1)

            def pool_projection(half):
                for t in range(HT):
                    for gg in range(2):
                        n = 8 * half + 2 * t + gg
                        if n == 4:
                            pe.wait_ge(diag_copied, 1)
                        at_least(pe, pool_added, n - 3)
                        for g in (2 * gg, 2 * gg + 1):
                            mm = three_passes(
                                DN[n % 4][:, (g % 2) * GROUP_DIM:(g % 2 + 1) * GROUP_DIM],
                                [(lambda q, c=2 * g + k: acts[half][:, q, c, t * P:(t + 1) * P],
                                  lambda q, r=2 * g + k: quad(POOL_Q, q, GROUP_DIM)[:, r, :]) for k in range(2)])
                        mm.then_inc(pool_full, 1)

            def up(layer, b, half):
                if half == 0:
                    pe.wait_ge(w_lo, 2 * (UP_Q[layer] + 2 * b) + 2)
                for f in range(2):
                    n = 4 * (NB * layer + b) + 2 * half + f
                    at_least(pe, up_sq, n - 1)
                    mm = three_passes(U[f][:, :], [
                        (lambda q, c=c: quad(UP_SLOT, q, FB)[:, c, f * P:(f + 1) * P],
                         lambda q, c=c: acts[half][:, q, c, :]) for c in range(DC)])
                    mm.then_inc(up_full, 1)

            def down(layer, b, half):
                if half == 0:
                    pe.wait_ge(w_lo, 2 * (UP_Q[layer] + 2 * b + 1) + 2)
                pe.wait_ge(up_lo, 4 * (NB * layer + b) + 2 * half + 2)
                for t in range(HT):
                    for dh in range(2):
                        i = 2 * t + dh
                        n = 16 * (NB * layer + b) + 8 * half + i
                        at_least(pe, down_added, n - 3)
                        mm = three_passes(DN[i % 4][:, :], [
                            (lambda q, f=f: squares[:, half, q, f, t * P:(t + 1) * P],
                             lambda q, f=f: quad(DOWN_SLOT, q, 512)[:, 2 * f + dh, :]) for f in range(2)])
                        mm.then_inc(down_full, 1)

            def mlp(layer, stage):
                up(layer, 0, 0)
                transposes(stage, 1)
                pe.wait_ge(t_lo, 16 * stage + 16)
                up(layer, 0, 1)
                down(layer, 0, 0)
                down(layer, 0, 1)
                with pe.Fori(1, NB) as b:
                    up(layer, b, 0)
                    up(layer, b, 1)
                    down(layer, b, 0)
                    down(layer, b, 1)

            pe.wait_ge(early_in, 16 * 4)
            pe.matmul(DN[0][0:N_HEADS, 0:N_DIAG], rel[:, :], one_hot[:, :], start=True, stop=True).then_inc(diag_full, 1)
            pe.wait_ge(consts_in, 16 * 9)
            pool_differences(0)
            pool_differences(1)
            pe.wait_ge(diag_copied, 1)
            pe.wait_ge(w_lo, 2)
            for half in range(2):
                pe.wait_ge(t_lo, 8 * half + 8)
                pool_projection(half)
            transposes(MLP0, 0)
            pe.wait_ge(t_lo, 16 * MLP0 + 8)
            mlp(0, MLP0)

            transposes(ATTN, 0)

            def keys(half):
                pe.wait_ge(w_lo, 2 * (KV_Q + 1) + 2)
                for i in range(2):
                    n = 2 * half + i
                    at_least(pe, kq_out, n - 1)
                    mm = three_passes(U[n % 2][:, :], [
                        (lambda q, c=c: kv_part(q, c)[:, i * P:(i + 1) * P],
                         lambda q, c=c: acts[half][:, q, c, :]) for c in range(DC)])
                    mm.then_inc(kq_full, 1)

            def values(half):
                for t in range(HT * half, HT * half + HT):
                    at_least(pe, vo_out, t - 1)
                    mm = three_passes(DN[t % 2][:, 0:KV_D], [
                        (lambda q, c=c: acts[half][:, q, c, (t % HT) * P:(t % HT + 1) * P],
                         lambda q, c=c: kv_part(q, c)[:, KV_D:2 * KV_D]) for c in range(DC)])
                    mm.then_inc(vo_full, 1)

            def query_tile(half, tile, chunks=range(DC)):
                n = 4 + 8 * half + tile
                j = Q_Q[half] + tile // 2
                if 0 in chunks:
                    pe.wait_ge(w_lo, 2 * j + 2)
                    pe.wait_ge(kq_out, n - 1)
                mm = three_passes(U[n % 2][:, :], [
                    (lambda q, c=c: quad(j, q, FB)[:, c, (tile % 2) * P:(tile % 2 + 1) * P],
                     lambda q, c=c: acts[half][:, q, c, :]) for c in chunks],
                    start=0 in chunks, stop=DC - 1 in chunks)
                if DC - 1 in chunks:
                    mm.then_inc(kq_full, 1)

            def output_bank(half, i, t):
                n = o_count(half, i, t)
                j = O_Q[half] + i
                pe.wait_ge(w_lo, 2 * j + 2)
                pe.wait_ge(vo_out, n - 1)
                if n == NT:
                    pe.wait_ge(logits_done, STEPS)
                pe.wait_ge(o_lo, 8 * half + 2 * t + 2)
                mm = three_passes(DN[n % 2][:, 0:FB], [
                    (lambda q, c=c: acts[half][:, q, c, t * P:(t + 1) * P],
                     lambda q, c=c: quad(j, q, FB)[:, c, :]) for c in range(DC)])
                mm.then_inc(vo_full, 1)

            pe.wait_ge(up_sq, 4 * NB)
            pe.wait_ge(down_added, 16 * NB)
            pe.wait_ge(t_lo, 16 * ATTN + 8)
            keys(0)
            transposes(ATTN, 1)
            values(0)
            pe.wait_ge(t_lo, 16 * ATTN + 16)
            keys(1)
            values(1)
            for tile in range(DC):
                query_tile(0, tile)

            def scores(a):
                half, n, i = a // STEPS, a // 2, a % 2
                if a == 0:
                    pe.wait_ge(pad_set, 2)
                pe.wait_ge(kq_out, 4 + 8 * half + 4 * i + 4)
                at_least(pe, logits_done, a - 1)
                if a == STEPS + 1:
                    pe.wait_ge(kq_out, 4 + 16)
                for s in range(2):
                    rows = slice(HEAD_DIM * s, HEAD_DIM * s + HEAD_DIM)
                    for p in range(2):
                        mm = pe.matmul(bank[score_banks(a) + s][:, p * P:(p + 1) * P],
                                       queries[half][rows, i, n % 8, 2 * p:2 * p + 2, :].rearrange(
                                           "p g t -> p (g t)"),
                                       kT[rows, i, CHUNK * n:CHUNK * n + BAND], start=True, stop=True)
                mm.then_inc(s_full, 1)

            def probs_transposed(a):
                pe.wait_ge(probs_done, a + 1)
                at_least(pe, pt_copied, a)
                for s in range(4):
                    mm = pe.transpose(PT[:, s * P:(s + 1) * P], probs[:, a % 2, s * P:(s + 1) * P], ident[:, :])
                mm.then_inc(pt_full, 1)

            def weighted_values(a):
                n, i = a // 2, a % 2
                pe.wait_ge(pt_copied, a + 1)
                if i == 0:
                    at_least(pe, o_lo, n)
                    half = a // STEPS
                    pe.wait_ge(shifted[half], 16 * (8 - half))
                source = v[:, n // 2, :] if n % 2 else v_shift[:, n // 2, :]
                for s in range(2):
                    k = 2 * i + s
                    mm = pe.matmul(PV[HEAD_DIM * s:HEAD_DIM * s + HEAD_DIM, i * 256:(i + 1) * 256],
                                   source[:, k * HEAD_DIM:(k + 1) * HEAD_DIM],
                                   probsT[:, a % 2, s * 256:(s + 1) * 256], start=True, stop=True)
                if i:
                    mm.then_inc(pv_full, 1)

            pe.wait_ge(vo_out, NT)
            scores(0)
            for a in range(2 * STEPS):
                if a + 1 < 2 * STEPS:
                    scores(a + 1)
                if a < STEPS:
                    chunks = range(0, 4) if a % 2 == 0 else range(4, DC)
                    query_tile(1, a // 2, chunks)
                else:
                    output_bank(0, (a - STEPS) // 4, a % 4)
                probs_transposed(a)
                weighted_values(a)
            for i in range(2):
                for t in range(HT):
                    output_bank(1, i, t)
            transposes(MLP1, 0)
            for i in range(2, 4):
                for t in range(HT):
                    output_bank(1, i, t)
            pe.wait_ge(t_lo, 16 * MLP1 + 8)
            mlp(1, MLP1)

        @block.vector
        def _(dve):
            steps = [0]

            def then_next(ins):
                steps[0] += 1
                ins.then_inc(dve_step, 1)
                dve.wait_ge(dve_step, steps[0])

            def normalise(stage, half):
                for t in range(HT * half, HT * half + HT):
                    dve.wait_ge(rstd_done, NT * stage + t + 1)
                    at_least(dve, t_full, 16 * stage + 8 * half)
                    dve.tensor_scalar(normed[:, t % HT, :], h[:, t, :], rstd[:, t:t + 1], None,
                                      ALU.mult).then_inc(normed_done, 1)

            def transposed_lo(stage, half, gain):
                for c in range(DC):
                    n = 16 * stage + 8 * half + c
                    dve.wait_ge(t_hi, n + 1)
                    hi = acts[half][:, 0, c, :].bitcast(F32)
                    if gain is None:
                        ins = dve.tensor_tensor(acts[half][:, 1, c, :], T[n % 2][:, :], hi, ALU.subtract)
                    else:
                        ins = dve.scalar_tensor_tensor(acts[half][:, 1, c, :], T[n % 2][:, :],
                                                       gains[:, gain, c:c + 1], hi, ALU.mult, ALU.subtract)
                    ins.then_inc(t_lo, 1)

            def split_lo(j, gain=None, n=QUAD, slot=None):
                slot = j % 2 if slot is None else slot
                for e in range(2):
                    dve.wait_ge(w_hi, 2 * j + e + 1)
                    if gain is None:
                        cols = slice(e * PIECE, (e + 1) * PIECE)
                        dve.tensor_tensor(wring[:, slot, 1, cols], wraw[:, e, :],
                                          wring[:, slot, 0, cols].bitcast(F32), ALU.subtract).then_inc(w_lo, 1)
                        continue
                    per = PIECE // n
                    for i in range(per):
                        c = (2 * ((j - KV_Q) * 2 + e) if n == 512 else 4 * e) + i
                        last = dve.scalar_tensor_tensor(
                            quad(j, 1, n)[:, per * e + i, :], wraw[:, e, i * n:(i + 1) * n],
                            gains[:, gain, c:c + 1], quad(j, 0, n)[:, per * e + i, :].bitcast(F32),
                            ALU.mult, ALU.subtract)
                    last.then_inc(w_lo, 1)

            def up_tile(layer, b, half, f):
                n = 4 * (NB * layer + b) + 2 * half + f
                dve.wait_ge(up_relu, n + 1)
                at_least(dve, up_hi, n - 1)
                dve.scalar_tensor_tensor(sq[:, f, :], U[f][:, :], 0.0, relu[:, f, :], ALU.max,
                                         ALU.mult).then_inc(up_sq, 1)
                dve.wait_ge(up_hi, n + 1)
                dve.tensor_tensor(squares[:, half, 1, f, :], sq[:, f, :],
                                  squares[:, half, 0, f, :].bitcast(F32), ALU.subtract).then_inc(up_lo, 1)

            def add_down(layer, b, half):
                for i in range(8):
                    n = 16 * (NB * layer + b) + 8 * half + i
                    dve.wait_ge(down_full, n + 1)
                    hs = h[:, HT * half + i // 2, (i % 2) * 512:(i % 2 + 1) * 512]
                    dve.tensor_tensor(hs, DN[i % 4][:, :], hs, ALU.add).then_inc(down_added, 1)

            def mlp_block(layer, b, after_first_half=None, next_up=True):
                split_lo(UP_Q[layer] + 2 * b + 1, slot=DOWN_SLOT)
                for f in range(2):
                    up_tile(layer, b, 0, f)
                if after_first_half:
                    after_first_half()
                for f in range(2):
                    up_tile(layer, b, 1, f)
                if next_up:
                    split_lo(UP_Q[layer] + 2 * b + 2, slot=UP_SLOT)
                add_down(layer, b, 0)
                if next_up:
                    add_down(layer, b, 1)

            def mlp(layer, stage, gain):
                def second_half():
                    transposed_lo(stage, 1, gain)
                mlp_block(layer, 0, second_half)
                with dve.Fori(1, NB - 1) as b:
                    mlp_block(layer, b)
                mlp_block(layer, NB - 1, next_up=False)

            normalise(POOLING, 0)
            dve.wait_ge(normed_done, HT)
            dve.tensor_copy(before[96:P, :], normed[96:P, HT - 1, :]).then_inc(before_done, 1)
            dve.wait_ge(early_in, 16 * 4)
            for e in range(2):
                dve.wait_ge(raw_in[e], 16)
                w = wraw[:, e, :].rearrange("p (g k d) -> p g k d", g=2, k=2)
                for g in range(2):
                    row = scale_row[:, (2 * e + g) * GROUP_DIM:(2 * e + g + 1) * GROUP_DIM]
                    for k in range(2):
                        last = dve.tensor_tensor(w[:, g, k, :], w[:, g, k, :], row, ALU.mult)
                last.then_inc(w_scaled, 1)
            dve.wait_ge(consts_in, 16 * 9)
            transposed_lo(POOLING, 0, 0)
            split_lo(POOL_Q)
            normalise(POOLING, 1)
            transposed_lo(POOLING, 1, 0)

            def add_pool(half):
                for i in range(8):
                    n = 8 * half + i
                    dve.wait_ge(pool_full, n + 1)
                    hs = h[:, HT * half + i // 2, (i % 2) * 512:(i % 2 + 1) * 512]
                    dve.tensor_tensor(hs, DN[n % 4][:, :], hs, ALU.add).then_inc(pool_added, 1)

            add_pool(0)
            add_pool(1)
            normalise(MLP0, 0)
            split_lo(UP_Q[0])
            transposed_lo(MLP0, 0, 2)
            normalise(MLP0, 1)
            mlp(0, MLP0, 2)

            split_lo(KV_Q, 4, 512)
            normalise(ATTN, 0)
            add_down(0, NB - 1, 1)
            transposed_lo(ATTN, 0, None)
            split_lo(KV_Q + 1, 4, 512)
            normalise(ATTN, 1)
            transposed_lo(ATTN, 1, None)
            for t in range(NT):
                dve.wait_ge(vo_full, t + 1)
                dve.tensor_tensor(v[:, t, :], DN[t % 2][:, 0:KV_D], bv_row[:, :], ALU.add).then_inc(vo_out, 1)
            for i in range(2 + 4):
                split_lo(Q_Q[0] + i, 1, FB)

            def logits(a):
                n, i, s = a // 2, a % 2, a % 2
                dve.wait_ge(s_full, a + 1)
                at_least(dve, pt_full, a - 1)
                at_least(dve, probs_done, a - 1)
                first = score_banks(a)
                then_next(dve.scalar_tensor_tensor(
                    probs[:, s, :].rearrange("p (a b) -> p a b", a=2), banks[:, first:first + 2, 0:2 * BAND],
                    HEAD_DIM ** -0.5, bias[:, 4 * i:4 * i + 4, :].rearrange("p (a c) b -> p a (c b)", a=2),
                    ALU.mult, ALU.add))
                last = probs[:, s, :].rearrange("p (a b) -> p a b", b=BAND)
                if n == 0:
                    then_next(dve.memset(last[:, :, 0:CHUNK], NEG_INF))
                then_next(dve.tensor_reduce(neg_max[:, s, :], last, AX.X, ALU.max, negate=True))
                then_next(dve.tensor_tensor(neg_max[:, s, :], neg_max[:, s, :],
                                            neg_sink[:, 4 * i:4 * i + 4], ALU.min))
                dve.tensor_tensor(sink_gap[:, s, :], neg_max[:, s, :], sink[:, 4 * i:4 * i + 4],
                                  ALU.add).then_inc(logits_done, 1)

            def softmax(a):
                s = a % 2
                dve.wait_ge(exp_done, a + 1)
                then_next(dve.tensor_tensor(denom[:, s, :], psum_row[:, s, :], sink_exp[:, s, :], ALU.add))
                then_next(dve.reciprocal(inv_denom[:, s, :], denom[:, s, :]))
                w = probs[:, s, :].rearrange("p (a b) -> p a b", b=BAND)
                dve.tensor_tensor(w, w, inv_denom[:, s, :].rearrange("p (a b) -> p a b", b=1).to_broadcast(
                    [P, 4, BAND]), ALU.mult).then_inc(probs_done, 1)

            def add_output(half, i, t):
                n = o_count(half, i, t)
                dve.wait_ge(vo_full, n + 1)
                hs = h[:, HT * half + t, i * FB:(i + 1) * FB]
                dve.tensor_tensor(hs, DN[n % 2][:, 0:FB], hs, ALU.add).then_inc(vo_out, 1)

            dve.wait_ge(bias_in, 32)
            dve.wait_ge(sink_neg, 1)
            logits(0)
            for a in range(2 * STEPS):
                half = a // STEPS
                if a + 1 < 2 * STEPS:
                    logits(a + 1)
                softmax(a)
                if half:
                    if a == STEPS:
                        dve.wait_ge(bo_added, NT)
                    add_output(0, (a - STEPS) // 4, a % 4)
                if a % 2:
                    n = a // 2
                    dve.wait_ge(o_hi, n + 1)
                    cols = slice(CHUNK * (n % 8), CHUNK * (n % 8) + CHUNK)
                    dve.tensor_tensor(acts[half][:, 1, :, cols], PV[:, :].rearrange("p (c t) -> p c t", t=CHUNK),
                                      acts[half][:, 0, :, cols].bitcast(F32), ALU.subtract).then_inc(o_lo, 1)
                if a % 4 == 3:
                    j = Q_Q[1] + a // 4 + 2
                    if j < O_Q[0]:
                        split_lo(j, 1, FB)
                    else:
                        split_lo(j)
            normalise(MLP1, 0)
            for i in range(4):
                for t in range(HT):
                    add_output(1, i, t)
                if i < 2:
                    split_lo(O_Q[1] + 2 + i)
                if i == 1:
                    transposed_lo(MLP1, 0, 3)
            split_lo(UP_Q[1])
            normalise(MLP1, 1)
            mlp(1, MLP1, 3)

            def final_norm(half):
                for t in range(HT * half, HT * half + HT):
                    dve.wait_ge(rstd_done, NT * FINAL + t + 1)
                    if half:
                        dve.wait_ge(out_done[t - HT], 16)
                    ins = dve.scalar_tensor_tensor(normed[:, t % HT, :], h[:, t, :], rstd[:, t:t + 1],
                                                   gf_row[:, :], ALU.mult, ALU.mult)
                    ins.then_inc(final_done, 1)

            dve.wait_ge(gf_in, 16)
            final_norm(0)
            add_down(1, NB - 1, 1)
            final_norm(1)


def kernel(**inputs):
    import numpy as _np
    import concourse.bacc as _bacc
    from concourse import mybir as _mybir
    from concourse.bass_utils import run_bass_kernel_spmd as _run

    a = {k: _np.asarray(v) for k, v in inputs.items()}

    def columns(g):
        return _np.moveaxis(g.reshape(*g.shape[:-1], DC, P), -1, 0)

    def pair_heads(w, axis):
        w = _np.moveaxis(w, axis, 0)
        w = w.reshape(2, 2, GROUP, HEAD_DIM, *w.shape[1:]).swapaxes(1, 2).reshape(w.shape)
        return _np.moveaxis(w, 0, axis)

    arrays = {
        "x": a["x"][0],
        "mix_g": columns(a["norm_mix_g"]),
        "mlp_g": columns(a["norm_mlp_g"]),
        "kv_g": columns(a["norm_kv_g"]),
        "pool_w": a["pool_w"][0],
        "pool_scale": a["pool_scale"][0],
        "w_kv": a["w_kv"],
        "b_k": a["b_kv"][:KV_D].reshape(2, P).T,
        "b_v": a["b_kv"][KV_D:],
        "w_q": pair_heads(a["w_q"][0], 1),
        "b_q": columns(pair_heads(a["b_q"][0], 0)),
        "sinks": a["sinks"][0].reshape(N_HEADS // 2, 2).T,
        "rel_bias": a["rel_bias"],
        "w_o": pair_heads(a["w_o"][0], 0),
        "b_o": a["b_o"][0],
        "w_up": a["w_up"],
        "w_down": a["w_down"],
        "norm_f_g": a["norm_f_g"],
        "bands": pool_bands(),
        "one_hot": t5_diagonals(),
        "ident": _np.eye(P, dtype=_np.float32),
    }
    nc = _bacc.Bacc("TRN2", target_bir_lowering=False, num_devices=1)
    feeds, args = {}, []
    for name, array in arrays.items():
        array = _np.ascontiguousarray(array)
        feeds[f"in_{name}"] = array
        args.append(nc.dram_tensor(f"in_{name}", array.shape, _mybir.dt.from_np(array.dtype),
                                   kind="ExternalInput").ap())
    args.append(nc.dram_tensor("out_y", (SEQ, D), _mybir.dt.float32, kind="ExternalOutput").ap())
    trunk(nc, *args)
    r = _run(nc, [feeds], core_ids=[0])
    return r.results[0]["out_y"].reshape(a["x"].shape)
```

```python
from contextlib import ExitStack

import concourse.bass as bass
import numpy as np
from concourse import mybir

F32 = mybir.dt.float32
F32R = mybir.dt.float32r
ALU = mybir.AluOpType
ACT = mybir.ActivationFunctionType
AX = mybir.AxisListType

P = 128
SEQ, D, D_FF = 1024, 1024, 4096
NT = SEQ // P
HALF = SEQ // 2
HT = HALF // P
DC = D // P
CHUNK, HEAD_DIM, N_HEADS, N_KV, GROUP = 64, 64, 16, 4, 4
BAND = 2 * CHUNK
KV_D = N_KV * HEAD_DIM
WINDOWS = (2, 4, 8, 16)
GROUP_DIM = D // len(WINDOWS)
N_BUCKETS, MAX_DISTANCE = 32, 128
N_DIAG = 192
EPS = 1e-6
NEG_INF = -1e30
FB = 256
NB = D_FF // FB
QUAD, PIECE = 2048, 1024

POOL_Q = 0
UP_Q = (1, 51)
KV_Q = 33
Q_Q = (35, 39)
O_Q = (43, 47)

UP_SLOT, DOWN_SLOT = 1, 0

POOLING, MLP0, ATTN, MLP1, FINAL = range(5)

STEPS = 16


def t5_diagonals():
    n = 127 - np.arange(N_DIAG - 1)
    half = N_BUCKETS // 2
    ret = (n < 0).astype(np.int32) * half
    n = np.abs(n)
    max_exact = half // 2
    large = max_exact + (np.log(np.maximum(n, 1) / max_exact)
                         / np.log(MAX_DISTANCE / max_exact) * (half - max_exact)).astype(np.int32)
    ret = ret + np.where(n < max_exact, n, np.minimum(large, half - 1))
    one_hot = np.zeros((N_BUCKETS, N_DIAG), np.float32)
    one_hot[ret, np.arange(N_DIAG - 1)] = 1.0
    return one_hot


def pool_bands():
    slabs = np.zeros((P, len(WINDOWS), 4, P), np.float32)
    first = np.zeros((P, len(WINDOWS), 2, 2, P), np.float32)
    t = np.arange(P)
    lag = t[None, :] - t[:, None]
    for g, w in enumerate(WINDOWS):
        inside = (lag >= 0) & (lag < w)
        slabs[:, g, 1] = inside / np.float32(w) - (lag == 0)
        slabs[:, g, 2] = (lag + P < w) / np.float32(w)
        whole = inside / np.minimum(t + 1, w).astype(np.float32)[None, :] - (lag == 0)
        whole = whole.astype(np.float32)
        high = (whole.view(np.uint32) & np.uint32(0xFFFFF000)).view(np.float32)
        first[:, g, 0, 0], first[:, g, 1, 0] = high, whole - high
        first[:, g, 0, 1] = slabs[:, g, 2]
    return slabs, first


def at_least(eng, sem, value):
    if not (isinstance(value, int) and value <= 0):
        eng.wait_ge(sem, value)


def trunk(nc, x, mix_g, mlp_g, kv_g, pool_w, pool_scale, w_kv, b_k, b_v, w_q, b_q, sinks, rel_bias,
          w_o, b_o, w_up, w_down, norm_f_g, slabs_in, first_in, one_hot_in, ident_in, out):
    ctx = ExitStack()
    with ctx:
        def sb(name, shape, dt=F32):
            return ctx.enter_context(nc.sbuf_tensor(name, shape, dt))

        def sem(name):
            return ctx.enter_context(nc.semaphore(name))

        h = sb("h", [P, NT, D])
        acts = [sb(f"acts{i}", [P, 2, DC, HALF], F32R) for i in range(2)]
        with nc.sbuf_tensor("normed_hi", [P, HT, D], F32R) as normed_hi:
            pass
        normed = sb("normed", [P, HT, D])
        wring = sb("wring", [P, 2, 2, QUAD], F32R)
        wraw = sb("wraw", [P, 2, PIECE])
        tmp_a = sb("tmp_a", [P, 2, 4, BAND + 4])
        tmp_b = sb("tmp_b", [P, 2, 512])
        ident = sb("ident", [P, P])
        gains = sb("gains", [P, 5, DC])
        bq_col = sb("bq_col", [P, DC])
        bk_col = sb("bk_col", [P, 2])
        bv_row = sb("bv_row", [P, KV_D])
        sink = sb("sink", [P, DC])
        neg_half = sb("neg_half", [P, 1])
        sumsq = sb("sumsq", [P, NT])
        variance = sb("variance", [P, NT])
        rstd = sb("rstd", [P, NT])
        neg_max = sb("neg_max", [P, 2, 4])
        denom = sb("denom", [P, 2, 4])
        inv_denom = sb("inv_denom", [P, 2, 4])

        with nc.sbuf_tensor("squares", [P, 2, 2, 2, 512], F32R) as squares:
            pass
        with nc.sbuf_tensor("normed_lo", [P, HT, D], F32R) as normed_lo:
            pass
        q1 = sb("q1", [P, 2, HALF // CHUNK, GROUP, CHUNK])
        with ExitStack() as early:
            def sb_early(name, shape, dt=F32):
                return early.enter_context(nc.sbuf_tensor(name, shape, dt))
            slabs = sb_early("slabs", [P, len(WINDOWS), 4 * P], F32R)
            first = sb_early("first", [P, len(WINDOWS), 2, 2 * P], F32R)
            before = sb_early("before", [P, 2, D], F32R)
            diag = sb_early("diag", [N_HEADS, N_DIAG])
            one_hot = sb_early("one_hot", [N_BUCKETS, N_DIAG])
            rel = sb_early("rel", [N_BUCKETS, N_HEADS])
        with nc.sbuf_tensor("gf_row", [P, D], F32) as gf_row:
            pass
        kT = sb("kT", [P, 2, CHUNK + SEQ])
        v = sb("v", [P, NT, KV_D])
        v_shift = sb("v_shift", [P, NT, KV_D])
        bias = sb("bias", [P, N_HEADS // 2, BAND])

        queries = [normed[:, :, :].rearrange("p a b -> p (a b)").rearrange(
            "p (i n g t) -> p i n g t", i=2, g=GROUP, t=CHUNK), q1[:, :, :, :, :]]
        flat_a = tmp_a[:, :, :, :].rearrange("p a b c -> p (a b c)")
        flat_b = tmp_b[:, :, :].rearrange("p a b -> p (a b)")
        relu = flat_a[:, 0:2 * 512].rearrange("p (a b) -> p a b", a=2)
        sq = tmp_b[:, :, :]
        probs, probsT = tmp_a, tmp_b[:, :, :]
        junk = flat_a[:, 0:D]
        scale_row, bo_row = flat_b, flat_b

        banks = ctx.enter_context(nc.psum_tensor("banks", [P, 8, 512], F32))
        bank = [banks[:, i, :] for i in range(8)]
        U = bank[0:2]
        DN = bank[2:6]
        T = bank[6:8]
        PT, PV = bank[4], bank[5]

        diag_dram = nc.dram_tensor("diag_dram", [N_HEADS, CHUNK, N_DIAG], F32, kind="Internal").ap()

        x_in = [sem(f"x_in{t}") for t in range(NT)]
        consts_in = sem("consts_in")
        early_in, rel_in = sem("early_in"), sem("rel_in")
        raw_in = [sem(f"raw_in{i}") for i in range(2)]
        w_hi, w_lo = sem("w_hi"), sem("w_lo")
        w_scaled = sem("w_scaled")
        ss_done, var_done, rstd_done = sem("ss_done"), sem("var_done"), sem("rstd_done")
        half_set = sem("half_set")
        nhi_done = sem("nhi_done")
        normed_done, before_done = sem("normed_done"), sem("before_done")
        t_full, t_hi, t_lo = sem("t_full"), sem("t_hi"), sem("t_lo")
        pool_full, pool_added = sem("pool_full"), sem("pool_added")
        diag_full, diag_copied, diag_out, bias_in = sem("diag_full"), sem("diag_copied"), sem("diag_out"), sem("bias_in")
        up_full, up_relu, up_sq, up_hi, up_lo = (sem(n) for n in ("up_full", "up_relu", "up_sq", "up_hi", "up_lo"))
        down_full, down_added = sem("down_full"), sem("down_added")
        kq_full, kq_out = sem("kq_full"), sem("kq_out")
        vo_full, vo_out = sem("vo_full"), sem("vo_out")
        shifted, pad_set = [sem(f"shifted{i}") for i in range(2)], sem("pad_set")
        bo_in, bo_added = sem("bo_in"), sem("bo_added")
        sink_in_probs = sem("sink_in_probs")
        s_full, logits_done, exp_done, probs_done = (
            sem(n) for n in ("s_full", "logits_done", "exp_done", "probs_done"))
        pt_full, pt_copied, pv_full, o_hi, o_lo = (
            sem(n) for n in ("pt_full", "pt_copied", "pv_full", "o_hi", "o_lo"))
        dve_step = sem("dve_step")
        gf_in, final_done = sem("gf_in"), sem("final_done")
        out_done = [sem(f"out_done{t}") for t in range(NT)]

        def quad(j, part, n):
            return wring[:, j % 2, part, :].rearrange("p (c n) -> p c n", n=n)

        def score_banks(a):
            return 6 if a % 2 == 0 else 2 if a < STEPS else 0

        def o_count(half, i, tt):
            return NT + 16 * half + 4 * i + tt

        block = ctx.enter_context(nc.Block())

        @block.sync
        def _(sp):
            x_tiles = x.rearrange("(t p) d -> t p d", p=P)
            out_tiles = out.rearrange("(t p) d -> t p d", p=P)
            pool_v = pool_w.rearrange("g (k p) d -> p g k d", p=P)
            kv_v = w_kv.rearrange("(c p) n -> p c n", p=P)
            q_v = w_q.rearrange("(c p) n -> p c n", p=P)
            o_v = w_o.rearrange("(c p) n -> p c n", p=P)
            up_v = [w_up[i].rearrange("(c p) n -> p c n", p=P) for i in range(2)]

            def load(j, e, source, n):
                at_least(sp, w_lo, 2 * j + e - 1)
                dst = wraw[:, e, :].rearrange("p (c n) -> p c n", n=n)
                sp.dma_start(dst, source).then_inc(raw_in[e], 16)

            def load_mlp(layer, b):
                for e in range(2):
                    load(UP_Q[layer] + 2 * b, e, up_v[layer][:, 4 * e:4 * e + 4, bass.ds(b * FB, FB)], FB)
                for e in range(2):
                    load(UP_Q[layer] + 2 * b + 1, e,
                         w_down[layer][bass.ds(b * FB + e * P, P), :].rearrange("p (c n) -> p c n", c=1), D)

            for t in range(HT):
                sp.dma_start(h[:, t, :], x_tiles[t]).then_inc(x_in[t], 16)
            for e in range(2):
                load(POOL_Q, e, pool_v[:, 2 * e:2 * e + 2].rearrange("p g k d -> p (g k) d"), GROUP_DIM)
            for t in range(HT, NT):
                sp.dma_start(h[:, t, :], x_tiles[t]).then_inc(x_in[t], 16)

            with sp.Fori(0, NB) as b:
                load_mlp(0, b)
            for i in range(2):
                for e in range(2):
                    load(KV_Q + i, e, kv_v[:, 4 * e:4 * e + 4, i * KV_D:(i + 1) * KV_D], KV_D)
            for base, view in ((Q_Q[0], q_v), (Q_Q[1], q_v), (O_Q[0], o_v), (O_Q[1], o_v)):
                for i in range(4):
                    for e in range(2):
                        load(base + i, e, view[:, 4 * e:4 * e + 4, i * FB:(i + 1) * FB], FB)
            with sp.Fori(0, NB) as b:
                load_mlp(1, b)

            for t in range(NT):
                sp.wait_ge(final_done, t + 1)
                sp.dma_start(out_tiles[t], normed[:, t % HT, :]).then_inc(out_done[t], 16)
            for t in range(NT):
                sp.wait_ge(out_done[t], 16)

        @block.gpsimd
        def _(pool):
            pool.memset(neg_half[:, :], -0.5).then_inc(half_set, 1)
            early_loads = [
                (slabs[:, :, :], slabs_in.rearrange("p g k t -> p g (k t)")),
                (first[:, :, :, :], first_in.rearrange("p g q k t -> p g q (k t)")),
                (scale_row, pool_scale.partition_broadcast(P)),
            ]
            for dst, src in early_loads:
                pool.dma_start(dst, src).then_inc(early_in, 16)
            pool.wait_ge(half_set, 1)

            def rstd_of(stage, tiles):
                for t in tiles:
                    n = NT * stage + t
                    pool.wait_ge(ss_done, n + 1)
                    at_least(pool, normed_done, n + 1 - NT)
                    pool.tensor_scalar(variance[:, t:t + 1], sumsq[:, t:t + 1], 1.0 / D, EPS,
                                       ALU.mult, ALU.add).then_inc(var_done, 1)
                    pool.wait_ge(var_done, n + 1)
                    pool.tensor_tensor(rstd[:, t:t + 1], variance[:, t:t + 1], neg_half[:, :],
                                       ALU.pow).then_inc(rstd_done, 1)

            half_tiles = [range(0, HT), range(HT, NT)]
            def scale_rows(j, gain):
                for e in range(2):
                    g = gains[:, gain, 4 * e:4 * e + 4].rearrange("p (c n) -> p c n", n=1)
                    w = wraw[:, e, :].rearrange("p (c n) -> p c n", n=FB)
                    pool.wait_ge(raw_in[e], 16 * (j + 1))
                    pool.tensor_tensor(w, w, g.to_broadcast([P, 4, FB]), ALU.mult).then_inc(w_scaled, 1)

            rstd_of(POOLING, half_tiles[0])
            pool.wait_ge(early_in, 16 * 3)
            for e in range(2):
                pool.wait_ge(raw_in[e], 16)
                w = wraw[:, e, :].rearrange("p (g k d) -> p g k d", g=2, k=2)
                for g in range(2):
                    row = scale_row[:, (2 * e + g) * GROUP_DIM:(2 * e + g + 1) * GROUP_DIM]
                    for k in range(2):
                        last = pool.tensor_tensor(w[:, g, k, :], w[:, g, k, :], row, ALU.mult)
                last.then_inc(w_scaled, 1)
            rstd_of(POOLING, half_tiles[1])
            pool.wait_ge(diag_copied, 1)
            pool.dma_start(diag_dram, diag[:, :].rearrange("h (a n) -> h a n", a=1).to_broadcast(
                [N_HEADS, CHUNK, N_DIAG])).then_inc(diag_out, 16)
            rstd_of(MLP0, half_tiles[0])
            rstd_of(MLP0, half_tiles[1])

            pool.wait_ge(pool_added, 2 * NT)
            pool.wait_ge(diag_out, 16)
            pool.memset(kT[:, :, 0:CHUNK], 0.0).then_inc(pad_set, 1)
            pool.memset(v_shift[0:CHUNK, 0, :], 0.0).then_inc(pad_set, 1)
            for i in range(2):
                rows = bass.AP(diag_dram.tensor, i * CHUNK * N_DIAG + CHUNK - 1,
                               [[N_DIAG - 1, CHUNK], [2 * CHUNK * N_DIAG, N_HEADS // 2], [1, BAND]])
                pool.dma_start(bias[CHUNK * i:CHUNK * i + CHUNK, :, :], rows).then_inc(bias_in, 16)
            pool.wait_ge(up_lo, 4 * NB)
            pool.wait_ge(up_hi, 4 * NB)
            pool.dma_start(bo_row, b_o.partition_broadcast(P)).then_inc(bo_in, 16)

            def add_bo(tiles):
                pool.wait_ge(bo_in, 16)
                for t in tiles:
                    pool.wait_ge(normed_done, NT * ATTN + t + 1)
                    pool.tensor_tensor(h[:, t, :], h[:, t, :], bo_row, ALU.add).then_inc(bo_added, 1)

            def shift_values(half):
                for t in half_tiles[half]:
                    pool.wait_ge(vo_out, t + 1)
                    pool.dma_start(v_shift[CHUNK:P, t, :], v[0:CHUNK, t, :]).then_inc(shifted[half], 16)
                    if t + 1 < NT:
                        pool.dma_start(v_shift[0:CHUNK, t + 1, :], v[CHUNK:P, t, :]).then_inc(shifted[half], 16)

            scale_rows(KV_Q, 4)
            rstd_of(ATTN, half_tiles[0])
            scale_rows(KV_Q + 1, 4)
            add_bo(half_tiles[0])
            rstd_of(ATTN, half_tiles[1])
            scale_rows(Q_Q[0], 1)
            add_bo(half_tiles[1])
            shift_values(0)
            shift_values(1)
            for i in range(1, 7):
                scale_rows(Q_Q[0] + i, 1)
            for a in range(2 * STEPS):
                at_least(pool, pt_full, a - 1)
                if a == 0:
                    pool.wait_ge(ss_done, NT * MLP1)
                pool.tensor_copy(probs[:, a % 2, :, BAND], sink[:, 4 * (a % 2):4 * (a % 2) + 4]).then_inc(
                    sink_in_probs, 1)
                if a == 6:
                    scale_rows(Q_Q[0] + 7, 1)
            rstd_of(MLP1, half_tiles[0])
            rstd_of(MLP1, half_tiles[1])
            pool.wait_ge(pv_full, SEQ // CHUNK)
            pool.dma_start(gf_row[:, :], norm_f_g.partition_broadcast(P)).then_inc(gf_in, 16)
            rstd_of(FINAL, half_tiles[0])
            rstd_of(FINAL, half_tiles[1])

        @block.scalar
        def _(act):
            act.dma_start(one_hot[:, :], one_hot_in).then_inc(rel_in, 16)
            act.dma_start(rel[:, :], rel_bias).then_inc(rel_in, 16)
            for dst, src in ((ident[:, :], ident_in), (gains[:, 0:2, :], mix_g), (gains[:, 2:4, :], mlp_g),
                             (gains[:, 4, :], kv_g), (bq_col[:, :], b_q), (bk_col[:, :], b_k),
                             (bv_row[:, :], b_v.partition_broadcast(P)),
                             (sink[0:CHUNK, :], sinks[0].partition_broadcast(CHUNK)),
                             (sink[CHUNK:P, :], sinks[1].partition_broadcast(CHUNK))):
                act.dma_start(dst, src).then_inc(consts_in, 16)

            def sum_squares(stage, half):
                for t in range(HT * half, HT * half + HT):
                    n = NT * stage + t
                    if stage == POOLING:
                        act.wait_ge(x_in[t], 16)
                    elif stage == MLP0:
                        act.wait_ge(pool_added, 2 * t + 2)
                    elif stage == ATTN or stage == FINAL:
                        layer = 0 if stage == ATTN else 1
                        act.wait_ge(down_added, 16 * NB * (layer + 1) - 2 * (NT - t) + 2)
                    else:
                        act.wait_ge(vo_out, o_count(half, 3, t % HT) + 1)
                    at_least(act, rstd_done, n + 1 - NT)
                    at_least(act, ss_done, n)
                    act.activation(junk, h[:, t, :], ACT.Square,
                                   accum_out=sumsq[:, t:t + 1]).then_inc(ss_done, 1)

            def transposed_hi(stage, half, gain, chunks=range(DC)):
                for c in chunks:
                    n = 16 * stage + 8 * half + c
                    act.wait_ge(t_full, n + 1)
                    scale = 1.0 if gain is None else gains[:, gain, c:c + 1]
                    act.activation(acts[half][:, 0, c, :], T[n % 2][:, :], ACT.Copy,
                                   scale=scale).then_inc(t_hi, 1)

            def projection_used(j):
                for half in range(2):
                    if Q_Q[half] <= j < Q_Q[half] + 4:
                        act.wait_ge(kq_full, 4 + 8 * half + 2 * (j - Q_Q[half]) + 2)
                    if O_Q[half] <= j < O_Q[half] + 4:
                        act.wait_ge(vo_full, o_count(half, j - O_Q[half], HT - 1) + 1)

            def split_hi(j, slot=None, scaled=None, pieces=range(2)):
                slot = j % 2 if slot is None else slot
                for e in pieces:
                    if scaled is not None:
                        act.wait_ge(w_scaled, scaled + e + 1)
                    else:
                        act.wait_ge(raw_in[e], 16 * (j + 1))
                    act.activation(wring[:, slot, 0, e * PIECE:(e + 1) * PIECE], wraw[:, e, :],
                                   ACT.Copy).then_inc(w_hi, 1)

            def up_tile(layer, b, half, f):
                n = 4 * (NB * layer + b) + 2 * half + f
                act.wait_ge(up_full, n + 1)
                at_least(act, up_sq, n - 1)
                act.activation(relu[:, f, :], U[f][:, :], ACT.Relu).then_inc(up_relu, 1)
                act.wait_ge(up_sq, n + 1)
                at_least(act, down_full, 16 * (NB * layer + b) + 8 * half - 8)
                act.activation(squares[:, half, 0, f, :], sq[:, f, :], ACT.Copy).then_inc(up_hi, 1)

            def mlp_block(layer, b, before_down=None, next_half=None, next_up=True):
                if before_down:
                    before_down()
                else:
                    act.wait_ge(down_full, 16 * (NB * layer + b))
                split_hi(UP_Q[layer] + 2 * b + 1, slot=DOWN_SLOT)
                for f in range(2):
                    if next_half:
                        next_half(range(2) if f == 0 else range(2, DC))
                    up_tile(layer, b, 0, f)
                for f in range(2):
                    up_tile(layer, b, 1, f)
                if next_up:
                    act.wait_ge(up_full, 4 * (NB * layer + b) + 4)
                    split_hi(UP_Q[layer] + 2 * b + 2, slot=UP_SLOT)

            def mlp(layer, stage, gain):
                def second_half(chunks):
                    transposed_hi(stage, 1, gain, chunks)
                act.wait_ge(ss_done, NT * (stage + 1))
                def down_slot_used():
                    if layer == 0:
                        act.wait_ge(pool_full, 2 * NT)
                    else:
                        projection_used(O_Q[1] + 3)
                mlp_block(layer, 0, down_slot_used, second_half)
                with act.Fori(1, NB - 1) as b:
                    mlp_block(layer, b)
                mlp_block(layer, NB - 1, next_up=False)

            def normed_high(half):
                for t in range(HT * half, HT * half + HT):
                    act.wait_ge(rstd_done, t + 1)
                    at_least(act, t_full, 8 * half)
                    act.activation(normed_hi[:, t % HT, :], h[:, t, :], ACT.Copy,
                                   scale=rstd[:, t:t + 1]).then_inc(nhi_done, 1)
                if half == 0:
                    act.wait_ge(nhi_done, HT)
                    act.activation(before[96:P, 0, :], normed_hi[96:P, HT - 1, :].bitcast(F32),
                                   ACT.Copy).then_inc(before_done, 1)

            sum_squares(POOLING, 0)
            normed_high(0)
            sum_squares(POOLING, 1)
            split_hi(POOL_Q, scaled=0)
            act.wait_ge(consts_in, 16 * 9)
            transposed_hi(POOLING, 0, 0)
            act.wait_ge(diag_full, 1)
            act.activation(diag[:, :], DN[3][0:N_HEADS, 0:N_DIAG], ACT.Copy).then_inc(diag_copied, 1)
            normed_high(1)
            transposed_hi(POOLING, 1, 0)
            split_hi(UP_Q[0])
            sum_squares(MLP0, 0)
            transposed_hi(MLP0, 0, 2)
            sum_squares(MLP0, 1)
            mlp(0, MLP0, 2)

            act.wait_ge(up_full, 4 * NB)
            split_hi(KV_Q, scaled=2)
            sum_squares(ATTN, 0)
            transposed_hi(ATTN, 0, None)
            act.wait_ge(down_full, 16 * NB)
            split_hi(KV_Q + 1, scaled=4)
            sum_squares(ATTN, 1)

            def key_out(half, i):
                act.wait_ge(kq_full, 2 * half + i + 1)
                act.activation(kT[:, i, CHUNK + HALF * half:CHUNK + HALF * half + HALF], U[i][:, :],
                               ACT.Identity, bias=bk_col[:, i:i + 1]).then_inc(kq_out, 1)

            def query_out(half, tile):
                n = 4 + 8 * half + tile
                act.wait_ge(kq_full, n + 1)
                act.activation(queries[half][:, tile // GROUP, :, tile % GROUP, :],
                               U[n % 2][:, :].rearrange("p (n t) -> p n t", t=CHUNK),
                               ACT.Identity, bias=bq_col[:, tile:tile + 1]).then_inc(kq_out, 1)

            act.wait_ge(pool_added, 2 * NT)
            act.wait_ge(diag_out, 16)
            transposed_hi(ATTN, 1, None)
            key_out(0, 0)
            key_out(0, 1)
            key_out(1, 0)
            key_out(1, 1)
            act.wait_ge(kq_full, 4)
            split_hi(Q_Q[0], scaled=6)
            act.wait_ge(vo_full, NT)
            split_hi(Q_Q[0] + 1, scaled=8)
            act.wait_ge(t_full, 16 * MLP1)
            for i in range(4):
                query_out(0, 2 * i)
                query_out(0, 2 * i + 1)
                projection_used(Q_Q[0] + i)
                split_hi(Q_Q[0] + 2 + i, scaled=10 + 2 * i)

            def exponentials(a):
                act.wait_ge(logits_done, a + 1)
                for s in range(4):
                    row = probs[:, a % 2, s, 0:BAND + 1]
                    last = act.activation(row, row, ACT.Exp, bias=neg_max[:, a % 2, s:s + 1],
                                          accum_out=denom[:, a % 2, s:s + 1])
                last.then_inc(exp_done, 1)

            exponentials(0)
            act.wait_ge(bo_added, NT)
            for a in range(2 * STEPS):
                half, step = a // STEPS, a % STEPS
                if a + 1 < 2 * STEPS:
                    exponentials(a + 1)
                if half == 0 and a % 2:
                    query_out(1, a // 2)
                act.wait_ge(pt_full, a + 1)
                at_least(act, pv_full, (a - 2) // 2 + 1 if a % 2 else (a - 2) // 2)
                act.activation(probsT[:, a % 2, :], PT[:, :], ACT.Copy).then_inc(pt_copied, 1)
                if a % 2:
                    n = a // 2
                    act.wait_ge(pv_full, n + 1)
                    act.activation(acts[half][:, 0, :, CHUNK * (n % 8):CHUNK * (n % 8) + CHUNK],
                                   PV[:, :].rearrange("p (c t) -> p c t", t=CHUNK), ACT.Copy).then_inc(o_hi, 1)
                if a % 4 == 3:
                    j = Q_Q[1] + a // 4 + 2
                    projection_used(j - 2)
                    split_hi(j, scaled=6 + 2 * (j - Q_Q[0]) if j < O_Q[0] else None, pieces=[0])
                elif a % 4 == 0 and a:
                    split_hi(j, scaled=6 + 2 * (j - Q_Q[0]) if j < O_Q[0] else None, pieces=[1])
            split_hi(O_Q[1] + 1, pieces=[1])
            sum_squares(MLP1, 0)
            for i in range(2):
                projection_used(O_Q[1] + i)
                split_hi(O_Q[1] + 2 + i)
            transposed_hi(MLP1, 0, 3)
            projection_used(O_Q[1] + 2)
            split_hi(UP_Q[1])
            sum_squares(MLP1, 1)
            mlp(1, MLP1, 3)
            sum_squares(FINAL, 0)
            sum_squares(FINAL, 1)

        @block.tensor
        def _(pe):
            def three_passes(dst, terms, start=True, stop=True, beside=None, first_bank=0):
                last_term = len(terms) - 1
                for i, (lhsT, rhs) in enumerate(terms):
                    pe.matmul(dst, lhsT(0), rhs(0), start=start and i == 0, stop=False)
                    pe.matmul(dst, lhsT(0), rhs(1), start=False, stop=False)
                    mm = pe.matmul(dst, lhsT(1), rhs(0), start=False, stop=stop and i == last_term)
                    if beside is not None and 0 <= first_bank + i < DC:
                        transpose_bank(beside, 1, first_bank + i)
                return mm

            def transpose_bank(stage, half, c):
                n = 16 * stage + 8 * half + c
                if c == 0:
                    pe.wait_ge(normed_done, NT * stage + HT * (half + 1))
                at_least(pe, t_lo, n - 1)
                for t in range(HT):
                    mm = pe.transpose(T[n % 2][:, t * P:(t + 1) * P], normed[:, t, c * P:(c + 1) * P],
                                      ident[:, :])
                mm.then_inc(t_full, 1)

            def pool_differences(half):
                pe.wait_ge(normed_done, HT * (half + 1))
                pe.wait_ge(before_done, 2 * half)
                for c in range(DC):
                    n = 8 * half + c
                    at_least(pe, t_lo, n - 1)
                    w = c * P // GROUP_DIM
                    cols = slice(c * P, (c + 1) * P)
                    dst = T[n % 2]

                    def token_tile(t, band, q, **flags):
                        source = normed_lo if q else normed_hi
                        at = min(t, HT - 2) * P
                        return pe.matmul(dst[:, at:at + 2 * P], source[:, t, cols], band, **flags)

                    if half == 0:
                        token_tile(0, first[:, w, 0, :], 0, start=True, stop=False)
                        token_tile(0, first[:, w, 1, :], 0, start=False, stop=False)
                        token_tile(0, first[:, w, 0, :], 1, start=False, stop=False)
                    else:
                        for q in range(2):
                            token_tile(0, slabs[:, w, P:3 * P], q, start=q == 0, stop=False)
                        for q in range(2):
                            pe.matmul(dst[:, 0:2 * P], before[96:P, q, cols], slabs[96:P, w, 2 * P:4 * P],
                                      start=False, stop=False)
                    for t in (2, 1, HT - 1):
                        band = slabs[:, w, 0:2 * P] if t == HT - 1 else slabs[:, w, P:3 * P]
                        for q in range(2):
                            mm = token_tile(t, band, q, start=False, stop=t == HT - 1 and q == 1)
                    mm.then_inc(t_full, 1)

            def pool_projection(half):
                pe.wait_ge(t_lo, 8 * half + 8)
                for t in range(HT):
                    for gg in range(2):
                        n = 8 * half + 2 * t + gg
                        if n == 3:
                            pe.wait_ge(diag_copied, 1)
                        at_least(pe, pool_added, n - 3)
                        for g in (2 * gg, 2 * gg + 1):
                            mm = three_passes(
                                DN[n % 4][:, (g % 2) * GROUP_DIM:(g % 2 + 1) * GROUP_DIM],
                                [(lambda q, c=2 * g + k: acts[half][:, q, c, t * P:(t + 1) * P],
                                  lambda q, r=2 * g + k: quad(POOL_Q, q, GROUP_DIM)[:, r, :]) for k in range(2)])
                        mm.then_inc(pool_full, 1)
                        if n >= 10:
                            transpose_bank(MLP0, 0, n - 10)

            def up(layer, b, half, next_half=None):
                if half == 0:
                    pe.wait_ge(w_lo, 2 * (UP_Q[layer] + 2 * b) + 2)
                for f in range(2):
                    n = 4 * (NB * layer + b) + 2 * half + f
                    at_least(pe, up_sq, n - 1)
                    mm = three_passes(U[f][:, :], [
                        (lambda q, c=c: quad(UP_SLOT, q, FB)[:, c, f * P:(f + 1) * P],
                         lambda q, c=c: acts[half][:, q, c, :]) for c in range(DC)],
                        beside=next_half, first_bank=DC * f - 6)
                    mm.then_inc(up_full, 1)

            def down(layer, b, half, next_norm=None):
                if half == 0:
                    pe.wait_ge(w_lo, 2 * (UP_Q[layer] + 2 * b + 1) + 2)
                pe.wait_ge(up_lo, 4 * (NB * layer + b) + 2 * half + 2)
                for t in range(HT):
                    for dh in range(2):
                        i = 2 * t + dh
                        n = 16 * (NB * layer + b) + 8 * half + i
                        at_least(pe, down_added, n - 3)
                        mm = three_passes(DN[i % 4][:, :], [
                            (lambda q, f=f: squares[:, half, q, f, t * P:(t + 1) * P],
                             lambda q, f=f: quad(DOWN_SLOT, q, 512)[:, 2 * f + dh, :]) for f in range(2)])
                        mm.then_inc(down_full, 1)
                        if next_norm is not None and i >= 4:
                            transpose_bank(next_norm, 0, 2 * (i - 4))
                            transpose_bank(next_norm, 0, 2 * (i - 4) + 1)

            def mlp(layer, stage, next_norm=None):
                up(layer, 0, 0, stage)
                pe.wait_ge(t_lo, 16 * stage + 16)
                up(layer, 0, 1)
                down(layer, 0, 0)
                down(layer, 0, 1)
                with pe.Fori(1, NB - 1) as b:
                    up(layer, b, 0)
                    up(layer, b, 1)
                    down(layer, b, 0)
                    down(layer, b, 1)
                up(layer, NB - 1, 0)
                up(layer, NB - 1, 1)
                down(layer, NB - 1, 0)
                down(layer, NB - 1, 1, next_norm)

            pe.wait_ge(early_in, 16 * 3)
            pool_differences(0)
            pe.wait_ge(rel_in, 16 * 2)
            pe.matmul(DN[3][0:N_HEADS, 0:N_DIAG], rel[:, :], one_hot[:, :], start=True, stop=True).then_inc(diag_full, 1)
            pe.wait_ge(w_lo, 2)
            pool_projection(0)
            pool_differences(1)
            pe.wait_ge(consts_in, 16 * 9)
            pool_projection(1)
            for c in (6, 7):
                transpose_bank(MLP0, 0, c)
            pe.wait_ge(t_lo, 16 * MLP0 + 8)
            mlp(0, MLP0, ATTN)

            def keys(half, beside=None):
                pe.wait_ge(w_lo, 2 * KV_Q + 2)
                for i in range(2):
                    n = 2 * half + i
                    at_least(pe, kq_out, n - 1)
                    mm = three_passes(U[n % 2][:, :], [
                        (lambda q, c=c: quad(KV_Q, q, KV_D)[:, c, i * P:(i + 1) * P],
                         lambda q, c=c: acts[half][:, q, c, :]) for c in range(DC)],
                        beside=beside, first_bank=DC * i - 4)
                    mm.then_inc(kq_full, 1)

            def values(half):
                pe.wait_ge(w_lo, 2 * (KV_Q + 1) + 2)
                for t in range(HT * half, HT * half + HT):
                    at_least(pe, vo_out, t - 1)
                    mm = three_passes(DN[t % 2][:, 0:KV_D], [
                        (lambda q, c=c: acts[half][:, q, c, (t % HT) * P:(t % HT + 1) * P],
                         lambda q, c=c: quad(KV_Q + 1, q, KV_D)[:, c, :]) for c in range(DC)])
                    mm.then_inc(vo_full, 1)

            def query_tile(half, tile, chunks=range(DC)):
                n = 4 + 8 * half + tile
                j = Q_Q[half] + tile // 2
                if 0 in chunks:
                    pe.wait_ge(w_lo, 2 * j + 2)
                    pe.wait_ge(kq_out, n - 1)
                mm = three_passes(U[n % 2][:, :], [
                    (lambda q, c=c: quad(j, q, FB)[:, c, (tile % 2) * P:(tile % 2 + 1) * P],
                     lambda q, c=c: acts[half][:, q, c, :]) for c in chunks],
                    start=0 in chunks, stop=DC - 1 in chunks)
                if DC - 1 in chunks:
                    mm.then_inc(kq_full, 1)

            def output_bank(half, i, t):
                n = o_count(half, i, t)
                j = O_Q[half] + i
                pe.wait_ge(w_lo, 2 * j + 2)
                pe.wait_ge(vo_out, n - 1)
                if n == NT:
                    pe.wait_ge(logits_done, STEPS)
                pe.wait_ge(o_lo, 8 * half + 2 * t + 2)
                mm = three_passes(DN[n % 2][:, 0:FB], [
                    (lambda q, c=c: acts[half][:, q, c, t * P:(t + 1) * P],
                     lambda q, c=c: quad(j, q, FB)[:, c, :]) for c in range(DC)])
                mm.then_inc(vo_full, 1)

            pe.wait_ge(up_sq, 4 * NB)
            pe.wait_ge(down_added, 16 * NB)
            pe.wait_ge(t_lo, 16 * ATTN + 8)
            keys(0, ATTN)
            values(0)
            pe.wait_ge(t_lo, 16 * ATTN + 16)
            keys(1)
            values(1)

            def scores(a):
                half, n, i = a // STEPS, a // 2, a % 2
                if a == 0:
                    pe.wait_ge(pad_set, 2)
                pe.wait_ge(kq_out, 4 + 8 * half + 4 * i + 4)
                at_least(pe, logits_done, a - 1)
                if a == STEPS + 1:
                    pe.wait_ge(kq_out, 4 + 16)
                for s in range(2):
                    rows = slice(HEAD_DIM * s, HEAD_DIM * s + HEAD_DIM)
                    for p in range(2):
                        mm = pe.matmul(bank[score_banks(a) + s][:, p * P:(p + 1) * P],
                                       queries[half][rows, i, n % 8, 2 * p:2 * p + 2, :].rearrange(
                                           "p g t -> p (g t)"),
                                       kT[rows, i, CHUNK * n:CHUNK * n + BAND], start=True, stop=True)
                mm.then_inc(s_full, 1)

            def probs_transposed(a):
                pe.wait_ge(probs_done, a + 1)
                at_least(pe, pt_copied, a)
                for s in range(4):
                    mm = pe.transpose(PT[:, s * P:(s + 1) * P], probs[:, a % 2, s, 0:BAND], ident[:, :])
                mm.then_inc(pt_full, 1)

            def weighted_values(a):
                n, i = a // 2, a % 2
                pe.wait_ge(pt_copied, a + 1)
                if i == 0:
                    at_least(pe, o_lo, n)
                    half = a // STEPS
                    pe.wait_ge(shifted[half], 16 * (8 - half))
                source = v[:, n // 2, :] if n % 2 else v_shift[:, n // 2, :]
                for s in range(2):
                    k = 2 * i + s
                    mm = pe.matmul(PV[HEAD_DIM * s:HEAD_DIM * s + HEAD_DIM, i * 256:(i + 1) * 256],
                                   source[:, k * HEAD_DIM:(k + 1) * HEAD_DIM],
                                   probsT[:, a % 2, s * 256:(s + 1) * 256], start=True, stop=True)
                if i:
                    mm.then_inc(pv_full, 1)

            for tile in range(DC):
                if tile == DC - 1:
                    pe.wait_ge(vo_out, NT)
                    scores(0)
                query_tile(0, tile)
            scores(1)
            for a in range(2 * STEPS):
                if a < STEPS:
                    chunks = range(0, 4) if a % 2 == 0 else range(4, DC)
                    query_tile(1, a // 2, chunks)
                else:
                    output_bank(0, (a - STEPS) // 4, a % 4)
                probs_transposed(a)
                if a + 2 < 2 * STEPS:
                    scores(a + 2)
                weighted_values(a)
            for i in range(4):
                for t in range(HT):
                    output_bank(1, i, t)
                    if i == 2:
                        transpose_bank(MLP1, 0, 2 * t)
                        transpose_bank(MLP1, 0, 2 * t + 1)
            pe.wait_ge(t_lo, 16 * MLP1 + 8)
            mlp(1, MLP1)

        @block.vector
        def _(dve):
            steps = [0]

            def then_next(ins):
                steps[0] += 1
                ins.then_inc(dve_step, 1)
                dve.wait_ge(dve_step, steps[0])

            def normalise(stage, half, tiles=range(HT)):
                for t in tiles:
                    t += HT * half
                    dve.wait_ge(rstd_done, NT * stage + t + 1)
                    at_least(dve, t_full, 16 * stage + 8 * half)
                    dve.tensor_scalar(normed[:, t % HT, :], h[:, t, :], rstd[:, t:t + 1], None,
                                      ALU.mult).then_inc(normed_done, 1)

            def transposed_lo(stage, half, gain, chunks=range(DC)):
                for c in chunks:
                    n = 16 * stage + 8 * half + c
                    dve.wait_ge(t_hi, n + 1)
                    hi = acts[half][:, 0, c, :].bitcast(F32)
                    if gain is None:
                        ins = dve.tensor_tensor(acts[half][:, 1, c, :], T[n % 2][:, :], hi, ALU.subtract)
                    else:
                        ins = dve.scalar_tensor_tensor(acts[half][:, 1, c, :], T[n % 2][:, :],
                                                       gains[:, gain, c:c + 1], hi, ALU.mult, ALU.subtract)
                    ins.then_inc(t_lo, 1)

            def split_lo(j, slot=None, pieces=range(2)):
                slot = j % 2 if slot is None else slot
                for e in pieces:
                    dve.wait_ge(w_hi, 2 * j + e + 1)
                    cols = slice(e * PIECE, (e + 1) * PIECE)
                    dve.tensor_tensor(wring[:, slot, 1, cols], wraw[:, e, :],
                                      wring[:, slot, 0, cols].bitcast(F32), ALU.subtract).then_inc(w_lo, 1)

            def up_tile(layer, b, half, f):
                n = 4 * (NB * layer + b) + 2 * half + f
                dve.wait_ge(up_relu, n + 1)
                at_least(dve, up_hi, n - 1)
                dve.scalar_tensor_tensor(sq[:, f, :], U[f][:, :], 0.0, relu[:, f, :], ALU.max,
                                         ALU.mult).then_inc(up_sq, 1)
                dve.wait_ge(up_hi, n + 1)
                dve.tensor_tensor(squares[:, half, 1, f, :], sq[:, f, :],
                                  squares[:, half, 0, f, :].bitcast(F32), ALU.subtract).then_inc(up_lo, 1)

            def add_down(layer, b, half, banks=range(8)):
                for i in banks:
                    n = 16 * (NB * layer + b) + 8 * half + i
                    dve.wait_ge(down_full, n + 1)
                    hs = h[:, HT * half + i // 2, (i % 2) * 512:(i % 2 + 1) * 512]
                    dve.tensor_tensor(hs, DN[i % 4][:, :], hs, ALU.add).then_inc(down_added, 1)

            def mlp_block(layer, b, next_half=None, next_up=True):
                split_lo(UP_Q[layer] + 2 * b + 1, slot=DOWN_SLOT)
                for f in range(2):
                    if next_half:
                        next_half(range(2) if f == 0 else range(2, DC))
                    up_tile(layer, b, 0, f)
                for f in range(2):
                    up_tile(layer, b, 1, f)
                if next_up:
                    add_down(layer, b, 0)
                    split_lo(UP_Q[layer] + 2 * b + 2, slot=UP_SLOT)
                    add_down(layer, b, 1)

            def mlp(layer, stage, gain):
                def second_half(chunks):
                    transposed_lo(stage, 1, gain, chunks)
                mlp_block(layer, 0, second_half)
                with dve.Fori(1, NB - 1) as b:
                    mlp_block(layer, b)
                mlp_block(layer, NB - 1, next_up=False)

            def normed_low(half):
                for t in range(HT * half, HT * half + HT):
                    dve.wait_ge(nhi_done, t + 1)
                    dve.scalar_tensor_tensor(normed_lo[:, t % HT, :], h[:, t, :], rstd[:, t:t + 1],
                                             normed_hi[:, t % HT, :].bitcast(F32), ALU.mult,
                                             ALU.subtract).then_inc(normed_done, 1)
                if half == 0:
                    dve.wait_ge(normed_done, HT)
                    dve.tensor_copy(before[96:P, 1, :],
                                    normed_lo[96:P, HT - 1, :].bitcast(F32)).then_inc(before_done, 1)

            normed_low(0)
            split_lo(POOL_Q)
            dve.wait_ge(consts_in, 16 * 9)
            transposed_lo(POOLING, 0, 0)

            def add_pool(half):
                for i in range(8):
                    n = 8 * half + i
                    dve.wait_ge(pool_full, n + 1)
                    hs = h[:, HT * half + i // 2, (i % 2) * 512:(i % 2 + 1) * 512]
                    dve.tensor_tensor(hs, DN[n % 4][:, :], hs, ALU.add).then_inc(pool_added, 1)
                    if n >= 10:
                        transposed_lo(MLP0, 0, 2, [n - 10])

            normed_low(1)
            add_pool(0)
            transposed_lo(POOLING, 1, 0)
            split_lo(UP_Q[0])
            normalise(MLP0, 0)
            add_pool(1)
            transposed_lo(MLP0, 0, 2, [6, 7])
            normalise(MLP0, 1)
            mlp(0, MLP0, 2)

            for t in range(HT):
                add_down(0, NB - 1, 0, (2 * t, 2 * t + 1))
                if t:
                    normalise(ATTN, 0, [t - 1])
            split_lo(KV_Q)
            for i in range(8):
                add_down(0, NB - 1, 1, [i])
                if i == 1:
                    normalise(ATTN, 0, [HT - 1])
                if i >= 4:
                    transposed_lo(ATTN, 0, None, (2 * (i - 4), 2 * (i - 4) + 1))
            split_lo(KV_Q + 1)
            normalise(ATTN, 1)
            transposed_lo(ATTN, 1, None)
            for t in range(NT):
                if t == NT - 1:
                    split_lo(Q_Q[0])
                dve.wait_ge(vo_full, t + 1)
                dve.tensor_tensor(v[:, t, :], DN[t % 2][:, 0:KV_D], bv_row[:, :], ALU.add).then_inc(vo_out, 1)
            for i in range(1, 2 + 4):
                split_lo(Q_Q[0] + i)

            def logits(a):
                n, i, s = a // 2, a % 2, a % 2
                dve.wait_ge(s_full, a + 1)
                at_least(dve, pt_full, a - 1)
                first_bank = score_banks(a)
                keys = probs[:, s, :, 0:BAND]
                for r in range(2):
                    last = dve.scalar_tensor_tensor(
                        keys[:, 2 * r:2 * r + 2, :],
                        bank[first_bank + r][:, 0:2 * BAND].rearrange("p (a b) -> p a b", b=BAND),
                        HEAD_DIM ** -0.5, bias[:, 4 * i + 2 * r:4 * i + 2 * r + 2, :], ALU.mult, ALU.add)
                then_next(last)
                if n == 0:
                    then_next(dve.memset(keys[:, :, 0:CHUNK], NEG_INF))
                dve.wait_ge(sink_in_probs, a + 1)
                dve.tensor_reduce(neg_max[:, s, :], probs[:, s, :, 0:BAND + 1], AX.X, ALU.max,
                                  negate=True).then_inc(logits_done, 1)

            def softmax(a):
                s = a % 2
                dve.wait_ge(exp_done, a + 1)
                then_next(dve.reciprocal(inv_denom[:, s, :], denom[:, s, :]))
                w = probs[:, s, :, 0:BAND]
                dve.tensor_tensor(w, w, inv_denom[:, s, :].rearrange("p (a b) -> p a b", b=1).to_broadcast(
                    [P, 4, BAND]), ALU.mult).then_inc(probs_done, 1)

            def add_output(half, i, t):
                n = o_count(half, i, t)
                dve.wait_ge(vo_full, n + 1)
                hs = h[:, HT * half + t, i * FB:(i + 1) * FB]
                dve.tensor_tensor(hs, DN[n % 2][:, 0:FB], hs, ALU.add).then_inc(vo_out, 1)

            dve.wait_ge(bias_in, 32)
            logits(0)
            for a in range(2 * STEPS):
                half = a // STEPS
                if a + 1 < 2 * STEPS:
                    logits(a + 1)
                softmax(a)
                if half:
                    if a == STEPS:
                        dve.wait_ge(bo_added, NT)
                    add_output(0, (a - STEPS) // 4, a % 4)
                if a % 2:
                    n = a // 2
                    dve.wait_ge(o_hi, n + 1)
                    cols = slice(CHUNK * (n % 8), CHUNK * (n % 8) + CHUNK)
                    dve.tensor_tensor(acts[half][:, 1, :, cols], PV[:, :].rearrange("p (c t) -> p c t", t=CHUNK),
                                      acts[half][:, 0, :, cols].bitcast(F32), ALU.subtract).then_inc(o_lo, 1)
                if a >= 4 and a % 4 < 2:
                    split_lo(Q_Q[1] + a // 4 + 1, pieces=[a % 4])
            split_lo(O_Q[1] + 1)
            normalise(MLP1, 0)
            for i in range(4):
                for t in range(HT):
                    add_output(1, i, t)
                    if i == 2:
                        transposed_lo(MLP1, 0, 3, (2 * t, 2 * t + 1))
                if i < 2:
                    split_lo(O_Q[1] + 2 + i)
            split_lo(UP_Q[1])
            normalise(MLP1, 1)
            mlp(1, MLP1, 3)

            def final_norm(tiles):
                for t in tiles:
                    dve.wait_ge(rstd_done, NT * FINAL + t + 1)
                    if t >= HT:
                        dve.wait_ge(out_done[t - HT], 16)
                    ins = dve.scalar_tensor_tensor(normed[:, t % HT, :], h[:, t, :], rstd[:, t:t + 1],
                                                   gf_row[:, :], ALU.mult, ALU.mult)
                    ins.then_inc(final_done, 1)

            dve.wait_ge(gf_in, 16)
            for t in range(HT):
                add_down(1, NB - 1, 0, (2 * t, 2 * t + 1))
                final_norm(range(t - 1, t) if t else [])
            for t in range(HT):
                add_down(1, NB - 1, 1, (2 * t, 2 * t + 1))
                final_norm([HT + t - 1])
            final_norm([NT - 1])


def kernel(**inputs):
    import numpy as _np
    import concourse.bacc as _bacc
    from concourse import mybir as _mybir
    from concourse.bass_utils import run_bass_kernel_spmd as _run

    a = {k: _np.asarray(v) for k, v in inputs.items()}

    def columns(g):
        return _np.moveaxis(g.reshape(*g.shape[:-1], DC, P), -1, 0)

    def pair_heads(w, axis):
        w = _np.moveaxis(w, axis, 0)
        w = w.reshape(2, 2, GROUP, HEAD_DIM, *w.shape[1:]).swapaxes(1, 2).reshape(w.shape)
        return _np.moveaxis(w, 0, axis)

    slabs, first = pool_bands()
    arrays = {
        "x": a["x"][0],
        "mix_g": columns(a["norm_mix_g"]),
        "mlp_g": columns(a["norm_mlp_g"]),
        "kv_g": columns(a["norm_kv_g"]),
        "pool_w": a["pool_w"][0],
        "pool_scale": a["pool_scale"][0],
        "w_kv": a["w_kv"],
        "b_k": a["b_kv"][:KV_D].reshape(2, P).T,
        "b_v": a["b_kv"][KV_D:],
        "w_q": pair_heads(a["w_q"][0], 1),
        "b_q": columns(pair_heads(a["b_q"][0], 0)),
        "sinks": a["sinks"][0].reshape(N_HEADS // 2, 2).T,
        "rel_bias": a["rel_bias"],
        "w_o": pair_heads(a["w_o"][0], 0),
        "b_o": a["b_o"][0],
        "w_up": a["w_up"],
        "w_down": a["w_down"],
        "norm_f_g": a["norm_f_g"],
        "slabs": slabs,
        "first": first,
        "one_hot": t5_diagonals(),
        "ident": _np.eye(P, dtype=_np.float32),
    }
    nc = _bacc.Bacc("TRN2", target_bir_lowering=False, num_devices=1)
    feeds, args = {}, []
    for name, array in arrays.items():
        array = _np.ascontiguousarray(array)
        feeds[f"in_{name}"] = array
        args.append(nc.dram_tensor(f"in_{name}", array.shape, _mybir.dt.from_np(array.dtype),
                                   kind="ExternalInput").ap())
    args.append(nc.dram_tensor("out_y", (SEQ, D), _mybir.dt.float32, kind="ExternalOutput").ap())
    trunk(nc, *args)
    r = _run(nc, [feeds], core_ids=[0])
    return r.results[0]["out_y"].reshape(a["x"].shape)
```

```python
from contextlib import ExitStack

import concourse.bass as bass
import numpy as np
from concourse import mybir

F32 = mybir.dt.float32
F32R = mybir.dt.float32r
ALU = mybir.AluOpType
ACT = mybir.ActivationFunctionType
AX = mybir.AxisListType

P = 128
SEQ, D, D_FF = 1024, 1024, 4096
NT = SEQ // P
HALF = SEQ // 2
HT = HALF // P
DC = D // P
CHUNK, HEAD_DIM, N_HEADS, N_KV, GROUP = 64, 64, 16, 4, 4
BAND = 2 * CHUNK
KV_D = N_KV * HEAD_DIM
WINDOWS = (2, 4, 8, 16)
GROUP_DIM = D // len(WINDOWS)
N_BUCKETS, MAX_DISTANCE = 32, 128
N_DIAG = 192
EPS = 1e-6
NEG_INF = -1e30
FB = 256
NB = D_FF // FB
QUAD, PIECE = 2048, 1024

POOL_Q = 0
UP_Q = (1, 51)
KV_Q = 33
Q_Q = (35, 39)
O_Q = (43, 47)

UP_SLOT, DOWN_SLOT = 1, 0

POOLING, MLP0, ATTN, MLP1, FINAL = range(5)

STEPS = 16


def t5_diagonals():
    n = 127 - np.arange(N_DIAG - 1)
    half = N_BUCKETS // 2
    ret = (n < 0).astype(np.int32) * half
    n = np.abs(n)
    max_exact = half // 2
    large = max_exact + (np.log(np.maximum(n, 1) / max_exact)
                         / np.log(MAX_DISTANCE / max_exact) * (half - max_exact)).astype(np.int32)
    ret = ret + np.where(n < max_exact, n, np.minimum(large, half - 1))
    one_hot = np.zeros((N_BUCKETS, N_DIAG), np.float32)
    one_hot[ret, np.arange(N_DIAG - 1)] = 1.0
    return one_hot


def pool_bands():
    slabs = np.zeros((P, len(WINDOWS), 4, P), np.float32)
    first = np.zeros((P, len(WINDOWS), 2, 2, P), np.float32)
    t = np.arange(P)
    lag = t[None, :] - t[:, None]
    for g, w in enumerate(WINDOWS):
        inside = (lag >= 0) & (lag < w)
        slabs[:, g, 1] = inside / np.float32(w) - (lag == 0)
        slabs[:, g, 2] = (lag + P < w) / np.float32(w)
        whole = inside / np.minimum(t + 1, w).astype(np.float32)[None, :] - (lag == 0)
        whole = whole.astype(np.float32)
        high = (whole.view(np.uint32) & np.uint32(0xFFFFF000)).view(np.float32)
        first[:, g, 0, 0], first[:, g, 1, 0] = high, whole - high
        first[:, g, 0, 1] = slabs[:, g, 2]
    return slabs, first


def at_least(eng, sem, value):
    if not (isinstance(value, int) and value <= 0):
        eng.wait_ge(sem, value)


def trunk(nc, x, mix_g, mlp_g, kv_g, pool_w, pool_scale, w_kv, b_k, b_v, w_q, b_q, sinks, rel_bias,
          w_o, b_o, w_up, w_down, norm_f_g, slabs_in, first_in, one_hot_in, ident_in, out):
    ctx = ExitStack()
    with ctx:
        def sb(name, shape, dt=F32):
            return ctx.enter_context(nc.sbuf_tensor(name, shape, dt))

        def sem(name):
            return ctx.enter_context(nc.semaphore(name))

        h = sb("h", [P, NT, D])
        acts = [sb(f"acts{i}", [P, 2, DC, HALF], F32R) for i in range(2)]
        with nc.sbuf_tensor("normed_hi", [P, HT, D], F32R) as normed_hi:
            pass
        normed = sb("normed", [P, HT, D])
        wring = sb("wring", [P, 2, 2, QUAD], F32R)
        wraw = sb("wraw", [P, 2, PIECE])
        tmp_a = sb("tmp_a", [P, 2, 4, BAND + 4])
        tmp_b = sb("tmp_b", [P, 2, 512])
        ident = sb("ident", [P, P])
        gains = sb("gains", [P, 5, DC])
        bq_col = sb("bq_col", [P, DC])
        bk_col = sb("bk_col", [P, 2])
        bv_row = sb("bv_row", [P, KV_D])
        sink = sb("sink", [P, DC])
        neg_half = sb("neg_half", [P, 1])
        sumsq = sb("sumsq", [P, NT])
        variance = sb("variance", [P, NT])
        rstd = sb("rstd", [P, NT])
        neg_max = sb("neg_max", [P, 2, 4])
        denom = sb("denom", [P, 2, 4])
        inv_denom = sb("inv_denom", [P, 2, 4])

        with nc.sbuf_tensor("squares", [P, 2, 2, 2, 512], F32R) as squares:
            pass
        with nc.sbuf_tensor("normed_lo", [P, HT, D], F32R) as normed_lo:
            pass
        q1 = sb("q1", [P, 2, HALF // CHUNK, GROUP, CHUNK])
        with ExitStack() as early:
            def sb_early(name, shape, dt=F32):
                return early.enter_context(nc.sbuf_tensor(name, shape, dt))
            slabs = sb_early("slabs", [P, len(WINDOWS), 4 * P], F32R)
            first = sb_early("first", [P, len(WINDOWS), 2, 2 * P], F32R)
            before = sb_early("before", [P, 2, D], F32R)
            diag = sb_early("diag", [N_HEADS, N_DIAG])
            one_hot = sb_early("one_hot", [N_BUCKETS, N_DIAG])
            rel = sb_early("rel", [N_BUCKETS, N_HEADS])
        with nc.sbuf_tensor("gf_row", [P, D], F32) as gf_row:
            pass
        kT = sb("kT", [P, 2, CHUNK + SEQ])
        v = sb("v", [P, NT, KV_D])
        v_shift = sb("v_shift", [P, NT, KV_D])
        bias = sb("bias", [P, N_HEADS // 2, BAND])

        queries = [normed[:, :, :].rearrange("p a b -> p (a b)").rearrange(
            "p (i n g t) -> p i n g t", i=2, g=GROUP, t=CHUNK), q1[:, :, :, :, :]]
        flat_a = tmp_a[:, :, :, :].rearrange("p a b c -> p (a b c)")
        flat_b = tmp_b[:, :, :].rearrange("p a b -> p (a b)")
        relu = flat_a[:, 0:2 * 512].rearrange("p (a b) -> p a b", a=2)
        sq = tmp_b[:, :, :]
        probs, probsT = tmp_a, tmp_b[:, :, :]
        junk = flat_a[:, 0:D]
        scale_row, bo_row = flat_b, flat_b

        banks = ctx.enter_context(nc.psum_tensor("banks", [P, 8, 512], F32))
        bank = [banks[:, i, :] for i in range(8)]
        U = bank[0:2]
        DN = bank[2:6]
        T = bank[6:8]
        PT, PV = bank[4], bank[5]

        diag_dram = nc.dram_tensor("diag_dram", [N_HEADS, CHUNK, N_DIAG], F32, kind="Internal").ap()

        x_in = [sem(f"x_in{t}") for t in range(NT)]
        consts_in = sem("consts_in")
        bands_in = [sem(f"bands_in{i}") for i in range(2)]
        scale_row_in, rel_in, mix_g_in = sem("scale_row_in"), sem("rel_in"), sem("mix_g_in")
        raw_in = [sem(f"raw_in{i}") for i in range(2)]
        w_hi, w_lo = sem("w_hi"), sem("w_lo")
        w_scaled = sem("w_scaled")
        ss_done, var_done, rstd_done = sem("ss_done"), sem("var_done"), sem("rstd_done")
        half_set = sem("half_set")
        nhi_done = sem("nhi_done")
        normed_done, before_done = sem("normed_done"), sem("before_done")
        t_full, t_hi, t_lo = sem("t_full"), sem("t_hi"), sem("t_lo")
        pool_full, pool_added = sem("pool_full"), sem("pool_added")
        diag_full, diag_copied, diag_out, bias_in = (
            sem(n) for n in ("diag_full", "diag_copied", "diag_out", "bias_in"))
        up_full, up_relu, up_sq, up_hi, up_lo = (sem(n) for n in ("up_full", "up_relu", "up_sq", "up_hi", "up_lo"))
        down_full, down_added = sem("down_full"), sem("down_added")
        kq_full, kq_out = sem("kq_full"), sem("kq_out")
        vo_full, vo_out = sem("vo_full"), sem("vo_out")
        shifted, pad_set = [sem(f"shifted{i}") for i in range(2)], sem("pad_set")
        bo_in, bo_added = sem("bo_in"), sem("bo_added")
        sink_in_probs = sem("sink_in_probs")
        s_full, logits_done, exp_done, probs_done = (
            sem(n) for n in ("s_full", "logits_done", "exp_done", "probs_done"))
        pt_full, pt_copied, pv_full, o_hi, o_lo = (
            sem(n) for n in ("pt_full", "pt_copied", "pv_full", "o_hi", "o_lo"))
        dve_step = sem("dve_step")
        gf_in, final_done = sem("gf_in"), sem("final_done")
        out_done = [sem(f"out_done{t}") for t in range(NT)]

        def quad(j, part, n):
            return wring[:, j % 2, part, :].rearrange("p (c n) -> p c n", n=n)

        def score_banks(a):
            return 6 if a % 2 == 0 else 2 if a < STEPS else 0

        def t_bank(n):
            return (T + U)[n % 4] if n < 2 * DC else T[n % 2]

        def mlp0_banks(n):
            return {10: [0], 11: [1, 2], 12: [3], 13: [4, 5], 14: [6], 15: [7]}.get(n, [])

        def o_count(half, i, tt):
            return NT + 16 * half + 4 * i + tt

        block = ctx.enter_context(nc.Block())

        @block.sync
        def _(sp):
            x_tiles = x.rearrange("(t p) d -> t p d", p=P)
            out_tiles = out.rearrange("(t p) d -> t p d", p=P)
            pool_v = pool_w.rearrange("g (k p) d -> p g k d", p=P)
            kv_v = w_kv.rearrange("(c p) n -> p c n", p=P)
            q_v = w_q.rearrange("(c p) n -> p c n", p=P)
            o_v = w_o.rearrange("(c p) n -> p c n", p=P)
            up_v = [w_up[i].rearrange("(c p) n -> p c n", p=P) for i in range(2)]

            def load(j, e, source, n):
                at_least(sp, w_lo, 2 * j + e - 1)
                dst = wraw[:, e, :].rearrange("p (c n) -> p c n", n=n)
                sp.dma_start(dst, source).then_inc(raw_in[e], 16)

            def load_mlp(layer, b):
                for e in range(2):
                    load(UP_Q[layer] + 2 * b, e, up_v[layer][:, 4 * e:4 * e + 4, bass.ds(b * FB, FB)], FB)
                for e in range(2):
                    load(UP_Q[layer] + 2 * b + 1, e,
                         w_down[layer][bass.ds(b * FB + e * P, P), :].rearrange("p (c n) -> p c n", c=1), D)

            for t in range(HT):
                sp.dma_start(h[:, t, :], x_tiles[t]).then_inc(x_in[t], 16)
            sp.dma_start(gains[:, 0:2, :], mix_g).then_inc(mix_g_in, 16)
            sp.dma_start(scale_row, pool_scale.partition_broadcast(P)).then_inc(scale_row_in, 16)
            for e in range(2):
                load(POOL_Q, e, pool_v[:, 2 * e:2 * e + 2].rearrange("p g k d -> p (g k) d"), GROUP_DIM)
            sp.dma_start(one_hot[:, :], one_hot_in).then_inc(rel_in, 16)
            sp.dma_start(rel[:, :], rel_bias).then_inc(rel_in, 16)
            for t in range(HT, NT):
                sp.dma_start(h[:, t, :], x_tiles[t]).then_inc(x_in[t], 16)
            for dst, src in ((ident[:, :], ident_in), (gains[:, 2:4, :], mlp_g), (gains[:, 4, :], kv_g),
                             (bq_col[:, :], b_q), (bk_col[:, :], b_k),
                             (bv_row[:, :], b_v.partition_broadcast(P)),
                             (sink[0:CHUNK, :], sinks[0].partition_broadcast(CHUNK)),
                             (sink[CHUNK:P, :], sinks[1].partition_broadcast(CHUNK))):
                sp.dma_start(dst, src).then_inc(consts_in, 16)

            with sp.Fori(0, NB) as b:
                load_mlp(0, b)
            for i in range(2):
                for e in range(2):
                    load(KV_Q + i, e, kv_v[:, 4 * e:4 * e + 4, i * KV_D:(i + 1) * KV_D], KV_D)
            for base, view in ((Q_Q[0], q_v), (Q_Q[1], q_v), (O_Q[0], o_v), (O_Q[1], o_v)):
                for i in range(4):
                    for e in range(2):
                        load(base + i, e, view[:, 4 * e:4 * e + 4, i * FB:(i + 1) * FB], FB)
            with sp.Fori(0, NB) as b:
                load_mlp(1, b)

            for t in range(NT):
                for e in range(2):
                    cols = slice(e * 512, (e + 1) * 512)
                    sp.wait_ge(final_done, 2 * t + e + 1)
                    sp.dma_start(out_tiles[t][:, cols], normed[:, t % HT, cols]).then_inc(out_done[t], 16)
            for t in range(NT):
                sp.wait_ge(out_done[t], 2 * 16)

        @block.gpsimd
        def _(pool):
            pool.memset(neg_half[:, :], -0.5).then_inc(half_set, 1)
            for i in range(2):
                w = slice(2 * i, 2 * i + 2)
                pool.dma_start(first[:, w, :, :], first_in[:, w].rearrange(
                    "p g q k t -> p g q (k t)")).then_inc(bands_in[i], 16)
                pool.dma_start(slabs[:, w, :], slabs_in[:, w].rearrange(
                    "p g k t -> p g (k t)")).then_inc(bands_in[i], 16)
            pool.wait_ge(half_set, 1)

            def rstd_of(stage, tiles):
                for t in tiles:
                    n = NT * stage + t
                    pool.wait_ge(ss_done, n + 1)
                    at_least(pool, normed_done, n + 1 - NT)
                    pool.tensor_scalar(variance[:, t:t + 1], sumsq[:, t:t + 1], 1.0 / D, EPS,
                                       ALU.mult, ALU.add).then_inc(var_done, 1)
                    pool.wait_ge(var_done, n + 1)
                    pool.tensor_tensor(rstd[:, t:t + 1], variance[:, t:t + 1], neg_half[:, :],
                                       ALU.pow).then_inc(rstd_done, 1)

            half_tiles = [range(0, HT), range(HT, NT)]

            def scale_rows(j, gain, pieces=range(2)):
                for e in pieces:
                    g = gains[:, gain, 4 * e:4 * e + 4].rearrange("p (c n) -> p c n", n=1)
                    w = wraw[:, e, :].rearrange("p (c n) -> p c n", n=FB)
                    pool.wait_ge(raw_in[e], 16 * (j + 1))
                    pool.tensor_tensor(w, w, g.to_broadcast([P, 4, FB]), ALU.mult).then_inc(w_scaled, 1)

            rstd_of(POOLING, half_tiles[0])
            pool.wait_ge(scale_row_in, 16)
            for e in range(2):
                pool.wait_ge(raw_in[e], 16)
                w = wraw[:, e, :].rearrange("p (g k d) -> p g k d", g=2, k=2)
                for g in range(2):
                    row = scale_row[:, (2 * e + g) * GROUP_DIM:(2 * e + g + 1) * GROUP_DIM]
                    for k in range(2):
                        last = pool.tensor_tensor(w[:, g, k, :], w[:, g, k, :], row, ALU.mult)
                last.then_inc(w_scaled, 1)
            rstd_of(POOLING, half_tiles[1])
            pool.wait_ge(diag_copied, 1)
            pool.dma_start(diag_dram, diag[:, :].rearrange("h (a n) -> h a n", a=1).to_broadcast(
                [N_HEADS, CHUNK, N_DIAG])).then_inc(diag_out, 16)
            rstd_of(MLP0, half_tiles[0])
            rstd_of(MLP0, half_tiles[1])

            pool.wait_ge(pool_added, 2 * NT)
            pool.wait_ge(diag_out, 16)
            pool.memset(kT[:, :, 0:CHUNK], 0.0).then_inc(pad_set, 1)
            pool.memset(v_shift[0:CHUNK, 0, :], 0.0).then_inc(pad_set, 1)
            for i in range(2):
                rows = bass.AP(diag_dram.tensor, i * CHUNK * N_DIAG + CHUNK - 1,
                               [[N_DIAG - 1, CHUNK], [2 * CHUNK * N_DIAG, N_HEADS // 2], [1, BAND]])
                pool.dma_start(bias[CHUNK * i:CHUNK * i + CHUNK, :, :], rows).then_inc(bias_in, 16)
            pool.wait_ge(up_lo, 4 * NB)
            pool.wait_ge(up_hi, 4 * NB)
            pool.dma_start(bo_row, b_o.partition_broadcast(P)).then_inc(bo_in, 16)

            def add_bo(tiles):
                pool.wait_ge(bo_in, 16)
                for t in tiles:
                    pool.wait_ge(normed_done, NT * ATTN + t + 1)
                    pool.tensor_tensor(h[:, t, :], h[:, t, :], bo_row, ALU.add).then_inc(bo_added, 1)

            def shift_values(half):
                for t in half_tiles[half]:
                    pool.wait_ge(vo_out, t + 1)
                    pool.dma_start(v_shift[CHUNK:P, t, :], v[0:CHUNK, t, :]).then_inc(shifted[half], 16)
                    if t + 1 < NT:
                        pool.dma_start(v_shift[0:CHUNK, t + 1, :], v[CHUNK:P, t, :]).then_inc(shifted[half], 16)

            scale_rows(KV_Q, 4)
            rstd_of(ATTN, half_tiles[0])
            scale_rows(KV_Q + 1, 4)
            rstd_of(ATTN, half_tiles[1])
            scale_rows(Q_Q[0], 1)
            add_bo(half_tiles[0])
            add_bo(half_tiles[1])
            shift_values(0)
            shift_values(1)

            def sink_column(a):
                at_least(pool, pt_full, a - 1)
                if a == 0:
                    pool.wait_ge(ss_done, NT * MLP1)
                pool.tensor_copy(probs[:, a % 2, :, BAND], sink[:, 4 * (a % 2):4 * (a % 2) + 4]).then_inc(
                    sink_in_probs, 1)

            sink_column(0)
            sink_column(1)
            for i in range(1, 6):
                scale_rows(Q_Q[0] + i, 1)
            for a in range(2, 2 * STEPS):
                sink_column(a)
                if a in (2, 3, 6, 7):
                    scale_rows(Q_Q[0] + 6 + a // 6, 1, [a % 2])
            rstd_of(MLP1, half_tiles[0])
            rstd_of(MLP1, half_tiles[1])
            pool.wait_ge(pv_full, SEQ // CHUNK)
            pool.dma_start(gf_row[:, :], norm_f_g.partition_broadcast(P)).then_inc(gf_in, 16)
            rstd_of(FINAL, half_tiles[0])
            rstd_of(FINAL, half_tiles[1])

        @block.scalar
        def _(act):
            def sum_squares(stage, half, tiles=range(HT)):
                for t in tiles:
                    t += HT * half
                    n = NT * stage + t
                    if stage == POOLING:
                        act.wait_ge(x_in[t], 16)
                    elif stage == MLP0:
                        act.wait_ge(pool_added, 2 * t + 2)
                    elif stage == ATTN or stage == FINAL:
                        layer = 0 if stage == ATTN else 1
                        act.wait_ge(down_added, 16 * NB * (layer + 1) - 2 * (NT - t) + 2)
                    else:
                        act.wait_ge(vo_out, o_count(half, 3, t % HT) + 1)
                    at_least(act, rstd_done, n + 1 - NT)
                    at_least(act, ss_done, n)
                    act.activation(junk, h[:, t, :], ACT.Square,
                                   accum_out=sumsq[:, t:t + 1]).then_inc(ss_done, 1)

            def transposed_hi(stage, half, gain, chunks=range(DC)):
                for c in chunks:
                    n = 16 * stage + 8 * half + c
                    act.wait_ge(t_full, n + 1)
                    scale = 1.0 if gain is None else gains[:, gain, c:c + 1]
                    act.activation(acts[half][:, 0, c, :], t_bank(n)[:, :], ACT.Copy,
                                   scale=scale).then_inc(t_hi, 1)

            def projection_used(j):
                for half in range(2):
                    if Q_Q[half] <= j < Q_Q[half] + 4:
                        act.wait_ge(kq_full, 4 + 8 * half + 2 * (j - Q_Q[half]) + 2)
                    if O_Q[half] <= j < O_Q[half] + 4:
                        act.wait_ge(vo_full, o_count(half, j - O_Q[half], HT - 1) + 1)

            def split_hi(j, slot=None, scaled=None, pieces=range(2)):
                slot = j % 2 if slot is None else slot
                for e in pieces:
                    if scaled is not None:
                        act.wait_ge(w_scaled, scaled + e + 1)
                    else:
                        act.wait_ge(raw_in[e], 16 * (j + 1))
                    act.activation(wring[:, slot, 0, e * PIECE:(e + 1) * PIECE], wraw[:, e, :],
                                   ACT.Copy).then_inc(w_hi, 1)

            def up_tile(layer, b, half, f):
                n = 4 * (NB * layer + b) + 2 * half + f
                act.wait_ge(up_full, n + 1)
                at_least(act, up_sq, n - 1)
                act.activation(relu[:, f, :], U[f][:, :], ACT.Relu).then_inc(up_relu, 1)
                act.wait_ge(up_sq, n + 1)
                at_least(act, down_full, 16 * (NB * layer + b) + 8 * half - 8)
                act.activation(squares[:, half, 0, f, :], sq[:, f, :], ACT.Copy).then_inc(up_hi, 1)

            def mlp_block(layer, b, before_down=None, next_half=None, next_up=True):
                if before_down:
                    before_down()
                else:
                    act.wait_ge(down_full, 16 * (NB * layer + b))
                split_hi(UP_Q[layer] + 2 * b + 1, slot=DOWN_SLOT)
                for f in range(2):
                    if next_half:
                        next_half(range(2) if f == 0 else range(2, DC))
                    up_tile(layer, b, 0, f)
                for f in range(2):
                    up_tile(layer, b, 1, f)
                if next_up:
                    act.wait_ge(up_full, 4 * (NB * layer + b) + 4)
                    split_hi(UP_Q[layer] + 2 * b + 2, slot=UP_SLOT)

            def mlp(layer, stage, gain):
                def second_half(chunks):
                    transposed_hi(stage, 1, gain, chunks)
                act.wait_ge(ss_done, NT * (stage + 1))
                def down_slot_used():
                    if layer == 0:
                        act.wait_ge(pool_full, 2 * NT)
                    else:
                        projection_used(O_Q[1] + 3)
                mlp_block(layer, 0, down_slot_used, second_half)
                with act.Fori(1, NB - 1) as b:
                    mlp_block(layer, b)
                mlp_block(layer, NB - 1, next_up=False)

            def normed_high(t):
                act.wait_ge(rstd_done, t + 1)
                at_least(act, t_full, t // HT * DC)
                act.activation(normed_hi[:, t % HT, :], h[:, t, :], ACT.Copy,
                               scale=rstd[:, t:t + 1]).then_inc(nhi_done, 1)

            def last_rows_high():
                act.wait_ge(nhi_done, HT)
                act.activation(before[96:P, 0, :], normed_hi[96:P, HT - 1, :].bitcast(F32),
                               ACT.Copy).then_inc(before_done, 1)

            for t in range(HT):
                sum_squares(POOLING, 0, [t])
                if t:
                    normed_high(t - 1)
            normed_high(HT - 1)
            last_rows_high()
            act.wait_ge(mix_g_in, 16)
            for c in range(DC):
                transposed_hi(POOLING, 0, 0, [c])
                if c in (4, 6):
                    split_hi(POOL_Q, scaled=0, pieces=[c // 2 - 2])
            act.wait_ge(diag_full, 1)
            act.activation(diag[:, :], DN[3][0:N_HEADS, 0:N_DIAG], ACT.Copy).then_inc(diag_copied, 1)
            for t in range(HT):
                sum_squares(POOLING, 1, [t])
                if t:
                    normed_high(HT + t - 1)
            normed_high(NT - 1)
            for c in range(DC):
                transposed_hi(POOLING, 1, 0, [c])
                if c % 2:
                    sum_squares(MLP0, 0, [c // 2])
            act.wait_ge(consts_in, 16 * 8)
            for n in range(NT, 2 * NT):
                transposed_hi(MLP0, 0, 2, mlp0_banks(n))
                if n in (12, 13):
                    split_hi(UP_Q[0], pieces=[n - 12])
                if n % 2:
                    sum_squares(MLP0, 1, [(n - NT) // 2])
            mlp(0, MLP0, 2)

            act.wait_ge(up_full, 4 * NB)
            sum_squares(ATTN, 0)
            split_hi(KV_Q, scaled=2)
            for t in range(HT):
                transposed_hi(ATTN, 0, None, (2 * t, 2 * t + 1))
                sum_squares(ATTN, 1, [t])
            act.wait_ge(down_full, 16 * NB)
            split_hi(KV_Q + 1, scaled=4)

            def key_out(half, i):
                act.wait_ge(kq_full, 2 * half + i + 1)
                act.activation(kT[:, i, CHUNK + HALF * half:CHUNK + HALF * half + HALF], U[i][:, :],
                               ACT.Identity, bias=bk_col[:, i:i + 1]).then_inc(kq_out, 1)

            def query_out(half, tile):
                n = 4 + 8 * half + tile
                act.wait_ge(kq_full, n + 1)
                act.activation(queries[half][:, tile // GROUP, :, tile % GROUP, :],
                               U[n % 2][:, :].rearrange("p (n t) -> p n t", t=CHUNK),
                               ACT.Identity, bias=bq_col[:, tile:tile + 1]).then_inc(kq_out, 1)

            act.wait_ge(pool_added, 2 * NT)
            act.wait_ge(diag_out, 16)
            transposed_hi(ATTN, 1, None)
            key_out(0, 0)
            key_out(0, 1)
            key_out(1, 0)
            key_out(1, 1)
            act.wait_ge(kq_full, 4)
            split_hi(Q_Q[0], scaled=6)
            act.wait_ge(vo_full, NT)
            split_hi(Q_Q[0] + 1, scaled=8)
            act.wait_ge(t_full, 16 * MLP1)
            for i in range(3):
                query_out(0, 2 * i)
                query_out(0, 2 * i + 1)
                projection_used(Q_Q[0] + i)
                split_hi(Q_Q[0] + 2 + i, scaled=10 + 2 * i)
            query_out(0, 6)

            def exponentials(a):
                act.wait_ge(logits_done, a + 1)
                for s in range(4):
                    row = probs[:, a % 2, s, 0:BAND + 1]
                    last = act.activation(row, row, ACT.Exp, bias=neg_max[:, a % 2, s:s + 1],
                                          accum_out=denom[:, a % 2, s:s + 1])
                last.then_inc(exp_done, 1)

            exponentials(0)
            query_out(0, 7)
            projection_used(Q_Q[0] + 3)
            split_hi(Q_Q[1] + 1, scaled=6 + 2 * (Q_Q[1] + 1 - Q_Q[0]), pieces=[0])
            act.wait_ge(bo_added, NT)
            for a in range(2 * STEPS):
                half = a // STEPS
                act.wait_ge(pt_full, a + 1)
                at_least(act, pv_full, a // 2)
                act.activation(probsT[:, a % 2, :], PT[:, :], ACT.Copy).then_inc(pt_copied, 1)
                if a + 1 < 2 * STEPS:
                    exponentials(a + 1)
                if half == 0 and a % 2:
                    query_out(1, a // 2)
                if a % 2:
                    n = a // 2
                    act.wait_ge(pv_full, n + 1)
                    act.activation(acts[half][:, 0, :, CHUNK * (n % 8):CHUNK * (n % 8) + CHUNK],
                                   PV[:, :].rearrange("p (c t) -> p c t", t=CHUNK), ACT.Copy).then_inc(o_hi, 1)
                j = Q_Q[1] + (a + 1) // 4 + 1
                if a % 4 == 3:
                    projection_used(j - 2)
                if a % 4 in (3, 0):
                    split_hi(j, scaled=6 + 2 * (j - Q_Q[0]) if j < O_Q[0] else None, pieces=[(a + 1) % 4])
            split_hi(O_Q[1] + 1, pieces=[1])
            sum_squares(MLP1, 0)
            for i in range(2):
                projection_used(O_Q[1] + i)
                split_hi(O_Q[1] + 2 + i)
            transposed_hi(MLP1, 0, 3)
            projection_used(O_Q[1] + 2)
            split_hi(UP_Q[1])
            sum_squares(MLP1, 1)
            mlp(1, MLP1, 3)
            sum_squares(FINAL, 0)
            sum_squares(FINAL, 1)

        @block.tensor
        def _(pe):
            def three_passes(dst, terms, start=True, stop=True, before=None, after=None):
                last_term = len(terms) - 1
                for i, (lhsT, rhs) in enumerate(terms):
                    if before:
                        before(i)
                    pe.matmul(dst, lhsT(0), rhs(0), start=start and i == 0, stop=False)
                    pe.matmul(dst, lhsT(0), rhs(1), start=False, stop=False)
                    mm = pe.matmul(dst, lhsT(1), rhs(0), start=False, stop=stop and i == last_term)
                    if after:
                        after(i)
                return mm

            def chunks_arrive(stage, half):
                return lambda c: pe.wait_ge(t_lo, 16 * stage + 8 * half + c + 1)

            def transpose_bank(stage, half, c):
                n = 16 * stage + 8 * half + c
                if c == 0:
                    pe.wait_ge(normed_done, NT * stage + HT * (half + 1))
                at_least(pe, t_lo, n - 1)
                for t in range(HT):
                    mm = pe.transpose(t_bank(n)[:, t * P:(t + 1) * P], normed[:, t, c * P:(c + 1) * P],
                                      ident[:, :])
                mm.then_inc(t_full, 1)

            def pool_differences(half):
                at_least(pe, before_done, 2 * half)
                for c in range(DC):
                    n = 8 * half + c
                    at_least(pe, t_lo, n - 3)
                    w = c * P // GROUP_DIM
                    if half == 0 and c % (DC // 2) == 0:
                        pe.wait_ge(bands_in[c // (DC // 2)], 16 * 2)
                    cols = slice(c * P, (c + 1) * P)
                    dst = t_bank(n)

                    def token_tile(t, band, q, **flags):
                        if c == 0:
                            pe.wait_ge(normed_done, HT * half + t + 1)
                        source = normed_lo if q else normed_hi
                        at = min(t, HT - 2) * P
                        return pe.matmul(dst[:, at:at + 2 * P], source[:, t, cols], band, **flags)

                    if half == 0:
                        token_tile(0, first[:, w, 0, :], 0, start=True, stop=False)
                        token_tile(0, first[:, w, 1, :], 0, start=False, stop=False)
                        token_tile(0, first[:, w, 0, :], 1, start=False, stop=False)
                    else:
                        for q in range(2):
                            token_tile(0, slabs[:, w, P:3 * P], q, start=q == 0, stop=False)
                        for q in range(2):
                            pe.matmul(dst[:, 0:2 * P], before[96:P, q, cols], slabs[96:P, w, 2 * P:4 * P],
                                      start=False, stop=False)
                    for t in (2, 1, HT - 1):
                        band = slabs[:, w, 0:2 * P] if t == HT - 1 else slabs[:, w, P:3 * P]
                        for q in range(2):
                            mm = token_tile(t, band, q, start=False, stop=t == HT - 1 and q == 1)
                    mm.then_inc(t_full, 1)

            def pool_projection(half):
                for t in range(HT):
                    for gg in range(2):
                        if t == 0:
                            pe.wait_ge(t_lo, 8 * half + 4 * gg + 4)
                            pe.wait_ge(w_lo, gg + 1)
                        n = 8 * half + 2 * t + gg
                        if n == 3:
                            pe.wait_ge(diag_copied, 1)
                        at_least(pe, pool_added, n - 3)
                        for g in (2 * gg, 2 * gg + 1):
                            mm = three_passes(
                                DN[n % 4][:, (g % 2) * GROUP_DIM:(g % 2 + 1) * GROUP_DIM],
                                [(lambda q, c=2 * g + k: acts[half][:, q, c, t * P:(t + 1) * P],
                                  lambda q, r=2 * g + k: quad(POOL_Q, q, GROUP_DIM)[:, r, :]) for k in range(2)])
                        mm.then_inc(pool_full, 1)
                        for c in mlp0_banks(n):
                            transpose_bank(MLP0, 0, c)

            def up(layer, b, half, stage=None):
                def second_half(f):
                    first_term = 6 if f == 0 else 2
                    bank_of = lambda i: i - first_term + 2 * f
                    return lambda i: transpose_bank(stage, 1, bank_of(i)) if i >= first_term else None

                if half == 0:
                    pe.wait_ge(w_lo, 2 * (UP_Q[layer] + 2 * b) + 2)
                for f in range(2):
                    n = 4 * (NB * layer + b) + 2 * half + f
                    at_least(pe, up_sq, n - 1)
                    mm = three_passes(U[f][:, :], [
                        (lambda q, c=c: quad(UP_SLOT, q, FB)[:, c, f * P:(f + 1) * P],
                         lambda q, c=c: acts[half][:, q, c, :]) for c in range(DC)],
                        before=chunks_arrive(stage, half) if stage is not None and f == 0 else None,
                        after=second_half(f) if stage is not None and half == 0 else None)
                    mm.then_inc(up_full, 1)

            def down(layer, b, half, next_norm=None):
                if half == 0:
                    pe.wait_ge(w_lo, 2 * (UP_Q[layer] + 2 * b + 1) + 2)
                pe.wait_ge(up_lo, 4 * (NB * layer + b) + 2 * half + 2)
                for t in range(HT):
                    for dh in range(2):
                        i = 2 * t + dh
                        n = 16 * (NB * layer + b) + 8 * half + i
                        at_least(pe, down_added, n - 3)
                        mm = three_passes(DN[i % 4][:, :], [
                            (lambda q, f=f: squares[:, half, q, f, t * P:(t + 1) * P],
                             lambda q, f=f: quad(DOWN_SLOT, q, 512)[:, 2 * f + dh, :]) for f in range(2)])
                        mm.then_inc(down_full, 1)
                        if next_norm is not None and i >= 4:
                            transpose_bank(next_norm, 0, 2 * (i - 4))
                            transpose_bank(next_norm, 0, 2 * (i - 4) + 1)

            def mlp(layer, stage, next_norm=None):
                up(layer, 0, 0, stage)
                up(layer, 0, 1, stage)
                down(layer, 0, 0)
                down(layer, 0, 1)
                with pe.Fori(1, NB - 1) as b:
                    up(layer, b, 0)
                    up(layer, b, 1)
                    down(layer, b, 0)
                    down(layer, b, 1)
                up(layer, NB - 1, 0)
                up(layer, NB - 1, 1)
                down(layer, NB - 1, 0)
                down(layer, NB - 1, 1, next_norm)

            pool_differences(0)
            pe.wait_ge(rel_in, 16 * 2)
            pe.matmul(DN[3][0:N_HEADS, 0:N_DIAG], rel[:, :], one_hot[:, :], start=True,
                      stop=True).then_inc(diag_full, 1)
            pool_projection(0)
            pool_differences(1)
            pe.wait_ge(consts_in, 16 * 8)
            pool_projection(1)
            mlp(0, MLP0, ATTN)

            def keys(half):
                def second_half(c):
                    if c in (4, 6):
                        transpose_bank(ATTN, 1, c // 2 - 2)

                pe.wait_ge(w_lo, 2 * KV_Q + 2)
                for i in range(2):
                    n = 2 * half + i
                    at_least(pe, kq_out, n - 1)
                    mm = three_passes(U[n % 2][:, :], [
                        (lambda q, c=c: quad(KV_Q, q, KV_D)[:, c, i * P:(i + 1) * P],
                         lambda q, c=c: acts[half][:, q, c, :]) for c in range(DC)],
                        before=chunks_arrive(ATTN, half) if i == 0 else None,
                        after=second_half if half == 0 and i == 1 else None)
                    mm.then_inc(kq_full, 1)

            def values(half):
                def second_half(t):
                    return lambda c: transpose_bank(ATTN, 1, 2 + 2 * t + c // 6) if c in (2, 6) else None

                pe.wait_ge(w_lo, 2 * (KV_Q + 1) + 2)
                for t in range(HT * half, HT * half + HT):
                    at_least(pe, vo_out, t - 1)
                    mm = three_passes(DN[t % 2][:, 0:KV_D], [
                        (lambda q, c=c: acts[half][:, q, c, (t % HT) * P:(t % HT + 1) * P],
                         lambda q, c=c: quad(KV_Q + 1, q, KV_D)[:, c, :]) for c in range(DC)],
                        after=second_half(t) if t < HT - 1 else None)
                    mm.then_inc(vo_full, 1)

            def query_tile(half, tile, chunks=range(DC)):
                n = 4 + 8 * half + tile
                j = Q_Q[half] + tile // 2
                if 0 in chunks:
                    pe.wait_ge(w_lo, 2 * j + 2)
                    pe.wait_ge(kq_out, n - 1)
                mm = three_passes(U[n % 2][:, :], [
                    (lambda q, c=c: quad(j, q, FB)[:, c, (tile % 2) * P:(tile % 2 + 1) * P],
                     lambda q, c=c: acts[half][:, q, c, :]) for c in chunks],
                    start=0 in chunks, stop=DC - 1 in chunks)
                if DC - 1 in chunks:
                    mm.then_inc(kq_full, 1)

            def output_bank(half, i, t):
                n = o_count(half, i, t)
                j = O_Q[half] + i
                pe.wait_ge(w_lo, 2 * j + 2)
                pe.wait_ge(vo_out, n - 1)
                if n == NT:
                    pe.wait_ge(logits_done, STEPS)
                pe.wait_ge(o_lo, 8 * half + 2 * t + 2)
                mm = three_passes(DN[n % 2][:, 0:FB], [
                    (lambda q, c=c: acts[half][:, q, c, t * P:(t + 1) * P],
                     lambda q, c=c: quad(j, q, FB)[:, c, :]) for c in range(DC)])
                mm.then_inc(vo_full, 1)

            pe.wait_ge(up_sq, 4 * NB)
            pe.wait_ge(down_added, 16 * NB)
            keys(0)
            values(0)
            keys(1)
            values(1)

            def scores(a):
                half, n, i = a // STEPS, a // 2, a % 2
                if a == 0:
                    pe.wait_ge(pad_set, 2)
                pe.wait_ge(kq_out, 4 + 8 * half + 4 * i + 4)
                at_least(pe, logits_done, a - 1)
                if a == STEPS + 1:
                    pe.wait_ge(kq_out, 4 + 16)
                for s in range(2):
                    rows = slice(HEAD_DIM * s, HEAD_DIM * s + HEAD_DIM)
                    for p in range(2):
                        mm = pe.matmul(bank[score_banks(a) + s][:, p * P:(p + 1) * P],
                                       queries[half][rows, i, n % 8, 2 * p:2 * p + 2, :].rearrange(
                                           "p g t -> p (g t)"),
                                       kT[rows, i, CHUNK * n:CHUNK * n + BAND], start=True, stop=True)
                mm.then_inc(s_full, 1)

            def probs_transposed(a):
                pe.wait_ge(probs_done, a + 1)
                at_least(pe, pt_copied, a)
                for s in range(4):
                    mm = pe.transpose(PT[:, s * P:(s + 1) * P], probs[:, a % 2, s, 0:BAND], ident[:, :])
                mm.then_inc(pt_full, 1)

            def weighted_values(a):
                n, i = a // 2, a % 2
                pe.wait_ge(pt_copied, a + 1)
                if i == 0:
                    at_least(pe, o_lo, n)
                    half = a // STEPS
                    pe.wait_ge(shifted[half], 16 * (8 - half))
                source = v[:, n // 2, :] if n % 2 else v_shift[:, n // 2, :]
                for s in range(2):
                    k = 2 * i + s
                    mm = pe.matmul(PV[HEAD_DIM * s:HEAD_DIM * s + HEAD_DIM, i * 256:(i + 1) * 256],
                                   source[:, k * HEAD_DIM:(k + 1) * HEAD_DIM],
                                   probsT[:, a % 2, s * 256:(s + 1) * 256], start=True, stop=True)
                if i:
                    mm.then_inc(pv_full, 1)

            for tile in range(DC):
                if tile == DC - 1:
                    pe.wait_ge(vo_out, NT)
                    scores(0)
                query_tile(0, tile)
            for a in range(2 * STEPS):
                if a < STEPS:
                    chunks = range(0, 4) if a % 2 == 0 else range(4, DC)
                    query_tile(1, a // 2, chunks)
                else:
                    output_bank(0, (a - STEPS) // 4, a % 4)
                if a in (0, STEPS):
                    scores(a + 1)
                probs_transposed(a)
                if a + 2 < 2 * STEPS and a + 2 != STEPS + 1:
                    scores(a + 2)
                weighted_values(a)
            for i in range(4):
                for t in range(HT):
                    output_bank(1, i, t)
                    if i == 2:
                        transpose_bank(MLP1, 0, 2 * t)
                        transpose_bank(MLP1, 0, 2 * t + 1)
            pe.wait_ge(t_lo, 16 * MLP1 + 8)
            mlp(1, MLP1)

        @block.vector
        def _(dve):
            steps = [0]

            def then_next(ins):
                steps[0] += 1
                ins.then_inc(dve_step, 1)
                dve.wait_ge(dve_step, steps[0])

            def normalise(stage, half, tiles=range(HT)):
                for t in tiles:
                    t += HT * half
                    dve.wait_ge(rstd_done, NT * stage + t + 1)
                    at_least(dve, t_full, 16 * stage + 8 * half)
                    dve.tensor_scalar(normed[:, t % HT, :], h[:, t, :], rstd[:, t:t + 1], None,
                                      ALU.mult).then_inc(normed_done, 1)

            def transposed_lo(stage, half, gain, chunks=range(DC)):
                for c in chunks:
                    n = 16 * stage + 8 * half + c
                    dve.wait_ge(t_hi, n + 1)
                    hi = acts[half][:, 0, c, :].bitcast(F32)
                    if gain is None:
                        ins = dve.tensor_tensor(acts[half][:, 1, c, :], t_bank(n)[:, :], hi, ALU.subtract)
                    else:
                        ins = dve.scalar_tensor_tensor(acts[half][:, 1, c, :], t_bank(n)[:, :],
                                                       gains[:, gain, c:c + 1], hi, ALU.mult, ALU.subtract)
                    ins.then_inc(t_lo, 1)

            def split_lo(j, slot=None, pieces=range(2)):
                slot = j % 2 if slot is None else slot
                for e in pieces:
                    dve.wait_ge(w_hi, 2 * j + e + 1)
                    cols = slice(e * PIECE, (e + 1) * PIECE)
                    dve.tensor_tensor(wring[:, slot, 1, cols], wraw[:, e, :],
                                      wring[:, slot, 0, cols].bitcast(F32), ALU.subtract).then_inc(w_lo, 1)

            def up_tile(layer, b, half, f):
                n = 4 * (NB * layer + b) + 2 * half + f
                dve.wait_ge(up_relu, n + 1)
                at_least(dve, up_hi, n - 1)
                dve.scalar_tensor_tensor(sq[:, f, :], U[f][:, :], 0.0, relu[:, f, :], ALU.max,
                                         ALU.mult).then_inc(up_sq, 1)
                dve.wait_ge(up_hi, n + 1)
                dve.tensor_tensor(squares[:, half, 1, f, :], sq[:, f, :],
                                  squares[:, half, 0, f, :].bitcast(F32), ALU.subtract).then_inc(up_lo, 1)

            def add_down(layer, b, half, banks=range(8)):
                for i in banks:
                    n = 16 * (NB * layer + b) + 8 * half + i
                    dve.wait_ge(down_full, n + 1)
                    hs = h[:, HT * half + i // 2, (i % 2) * 512:(i % 2 + 1) * 512]
                    dve.tensor_tensor(hs, DN[i % 4][:, :], hs, ALU.add).then_inc(down_added, 1)

            def mlp_block(layer, b, next_half=None, next_up=True):
                split_lo(UP_Q[layer] + 2 * b + 1, slot=DOWN_SLOT)
                for f in range(2):
                    if next_half:
                        next_half(range(2) if f == 0 else range(2, DC))
                    up_tile(layer, b, 0, f)
                for f in range(2):
                    up_tile(layer, b, 1, f)
                if next_up:
                    add_down(layer, b, 0)
                    split_lo(UP_Q[layer] + 2 * b + 2, slot=UP_SLOT)
                    add_down(layer, b, 1)

            def mlp(layer, stage, gain):
                def second_half(chunks):
                    transposed_lo(stage, 1, gain, chunks)
                mlp_block(layer, 0, second_half)
                with dve.Fori(1, NB - 1) as b:
                    mlp_block(layer, b)
                mlp_block(layer, NB - 1, next_up=False)

            def normed_low(t):
                dve.wait_ge(nhi_done, t + 1)
                dve.scalar_tensor_tensor(normed_lo[:, t % HT, :], h[:, t, :], rstd[:, t:t + 1],
                                         normed_hi[:, t % HT, :].bitcast(F32), ALU.mult,
                                         ALU.subtract).then_inc(normed_done, 1)

            for t in range(HT):
                normed_low(t)
            dve.wait_ge(normed_done, HT)
            dve.tensor_copy(before[96:P, 1, :],
                            normed_lo[96:P, HT - 1, :].bitcast(F32)).then_inc(before_done, 1)
            dve.wait_ge(mix_g_in, 16)
            for c in range(DC):
                transposed_lo(POOLING, 0, 0, [c])
                if c in (4, 6):
                    split_lo(POOL_Q, pieces=[c // 2 - 2])

            def add_pool(n):
                dve.wait_ge(pool_full, n + 1)
                hs = h[:, n // 2, (n % 2) * 512:(n % 2 + 1) * 512]
                dve.tensor_tensor(hs, DN[n % 4][:, :], hs, ALU.add).then_inc(pool_added, 1)

            for t in range(HT):
                normed_low(HT + t)
                add_pool(2 * t)
                add_pool(2 * t + 1)
            transposed_lo(POOLING, 1, 0)
            normalise(MLP0, 0)
            dve.wait_ge(consts_in, 16 * 8)
            for n in range(NT, 2 * NT):
                add_pool(n)
                transposed_lo(MLP0, 0, 2, mlp0_banks(n))
                if n in (12, 13):
                    split_lo(UP_Q[0], pieces=[n - 12])
            normalise(MLP0, 1)
            mlp(0, MLP0, 2)

            for t in range(HT):
                add_down(0, NB - 1, 0, (2 * t, 2 * t + 1))
                if t:
                    normalise(ATTN, 0, [t - 1])
            for i in range(8):
                add_down(0, NB - 1, 1, [i])
                if i == 1:
                    normalise(ATTN, 0, [HT - 1])
                if i in (2, 3):
                    split_lo(KV_Q, pieces=[i - 2])
                if i >= 4:
                    transposed_lo(ATTN, 0, None, (2 * (i - 4), 2 * (i - 4) + 1))
            normalise(ATTN, 1)
            split_lo(KV_Q + 1)
            transposed_lo(ATTN, 1, None, (0, 1))
            for t in range(NT):
                if t < HT - 1:
                    transposed_lo(ATTN, 1, None, (2 + 2 * t, 3 + 2 * t))
                if t == NT - 1:
                    split_lo(Q_Q[0])
                dve.wait_ge(vo_full, t + 1)
                dve.tensor_tensor(v[:, t, :], DN[t % 2][:, 0:KV_D], bv_row[:, :], ALU.add).then_inc(vo_out, 1)
            for i in range(1, 1 + 4):
                split_lo(Q_Q[0] + i)

            def logits(a):
                n, i, s = a // 2, a % 2, a % 2
                dve.wait_ge(s_full, a + 1)
                at_least(dve, pt_full, a - 1)
                first_bank = score_banks(a)
                keys = probs[:, s, :, 0:BAND]
                for r in range(2):
                    last = dve.scalar_tensor_tensor(
                        keys[:, 2 * r:2 * r + 2, :],
                        bank[first_bank + r][:, 0:2 * BAND].rearrange("p (a b) -> p a b", b=BAND),
                        HEAD_DIM ** -0.5, bias[:, 4 * i + 2 * r:4 * i + 2 * r + 2, :], ALU.mult, ALU.add)
                then_next(last)
                if n == 0:
                    then_next(dve.memset(keys[:, :, 0:CHUNK], NEG_INF))
                dve.wait_ge(sink_in_probs, a + 1)
                dve.tensor_reduce(neg_max[:, s, :], probs[:, s, :, 0:BAND + 1], AX.X, ALU.max,
                                  negate=True).then_inc(logits_done, 1)

            def softmax(a):
                s = a % 2
                dve.wait_ge(exp_done, a + 1)
                then_next(dve.reciprocal(inv_denom[:, s, :], denom[:, s, :]))
                w = probs[:, s, :, 0:BAND]
                dve.tensor_tensor(w, w, inv_denom[:, s, :].rearrange("p (a b) -> p a b", b=1).to_broadcast(
                    [P, 4, BAND]), ALU.mult).then_inc(probs_done, 1)

            def add_output(half, i, t):
                n = o_count(half, i, t)
                dve.wait_ge(vo_full, n + 1)
                hs = h[:, HT * half + t, i * FB:(i + 1) * FB]
                dve.tensor_tensor(hs, DN[n % 2][:, 0:FB], hs, ALU.add).then_inc(vo_out, 1)

            dve.wait_ge(bias_in, 32)
            logits(0)
            def attention_lo(a):
                half, n = a // STEPS, a // 2
                dve.wait_ge(o_hi, n + 1)
                cols = slice(CHUNK * (n % 8), CHUNK * (n % 8) + CHUNK)
                dve.tensor_tensor(acts[half][:, 1, :, cols], PV[:, :].rearrange("p (c t) -> p c t", t=CHUNK),
                                  acts[half][:, 0, :, cols].bitcast(F32), ALU.subtract).then_inc(o_lo, 1)

            for a in range(2 * STEPS):
                if a % 4 in (1, 2):
                    split_lo(Q_Q[1] + a // 4 + 1, pieces=[a % 4 - 1])
                if a > STEPS:
                    if a == STEPS + 1:
                        dve.wait_ge(bo_added, NT)
                    add_output(0, (a - 1 - STEPS) // 4, (a - 1) % 4)
                softmax(a)
                if a and a % 2 == 0:
                    attention_lo(a - 1)
                if a + 1 < 2 * STEPS:
                    logits(a + 1)
            add_output(0, 3, 3)
            attention_lo(2 * STEPS - 1)
            split_lo(O_Q[1] + 1)
            for i in range(4):
                for t in range(HT):
                    add_output(1, i, t)
                    if i == 0:
                        normalise(MLP1, 0, [t])
                    if i == 2:
                        transposed_lo(MLP1, 0, 3, (2 * t, 2 * t + 1))
                    if i == 3 and t in (1, 2):
                        split_lo(UP_Q[1], pieces=[t - 1])
                if i < 2:
                    split_lo(O_Q[1] + 2 + i)
            normalise(MLP1, 1)
            mlp(1, MLP1, 3)

            def final_norm(tiles):
                for t in tiles:
                    dve.wait_ge(rstd_done, NT * FINAL + t + 1)
                    if t >= HT:
                        dve.wait_ge(out_done[t - HT], 2 * 16)
                    for e in range(2):
                        cols = slice(e * 512, (e + 1) * 512)
                        dve.scalar_tensor_tensor(normed[:, t % HT, cols], h[:, t, cols], rstd[:, t:t + 1],
                                                 gf_row[:, cols], ALU.mult, ALU.mult).then_inc(final_done, 1)

            dve.wait_ge(gf_in, 16)
            for t in range(HT):
                add_down(1, NB - 1, 0, (2 * t, 2 * t + 1))
                final_norm(range(t - 1, t) if t else [])
            for t in range(HT):
                add_down(1, NB - 1, 1, (2 * t, 2 * t + 1))
                final_norm([HT + t - 1])
            final_norm([NT - 1])


def kernel(**inputs):
    import numpy as _np
    import concourse.bacc as _bacc
    from concourse import mybir as _mybir
    from concourse.bass_utils import run_bass_kernel_spmd as _run

    a = {k: _np.asarray(v) for k, v in inputs.items()}

    def columns(g):
        return _np.moveaxis(g.reshape(*g.shape[:-1], DC, P), -1, 0)

    def pair_heads(w, axis):
        w = _np.moveaxis(w, axis, 0)
        w = w.reshape(2, 2, GROUP, HEAD_DIM, *w.shape[1:]).swapaxes(1, 2).reshape(w.shape)
        return _np.moveaxis(w, 0, axis)

    slabs, first = pool_bands()
    arrays = {
        "x": a["x"][0],
        "mix_g": columns(a["norm_mix_g"]),
        "mlp_g": columns(a["norm_mlp_g"]),
        "kv_g": columns(a["norm_kv_g"]),
        "pool_w": a["pool_w"][0],
        "pool_scale": a["pool_scale"][0],
        "w_kv": a["w_kv"],
        "b_k": a["b_kv"][:KV_D].reshape(2, P).T,
        "b_v": a["b_kv"][KV_D:],
        "w_q": pair_heads(a["w_q"][0], 1),
        "b_q": columns(pair_heads(a["b_q"][0], 0)),
        "sinks": a["sinks"][0].reshape(N_HEADS // 2, 2).T,
        "rel_bias": a["rel_bias"],
        "w_o": pair_heads(a["w_o"][0], 0),
        "b_o": a["b_o"][0],
        "w_up": a["w_up"],
        "w_down": a["w_down"],
        "norm_f_g": a["norm_f_g"],
        "slabs": slabs,
        "first": first,
        "one_hot": t5_diagonals(),
        "ident": _np.eye(P, dtype=_np.float32),
    }
    nc = _bacc.Bacc("TRN2", target_bir_lowering=False, num_devices=1)
    feeds, args = {}, []
    for name, array in arrays.items():
        array = _np.ascontiguousarray(array)
        feeds[f"in_{name}"] = array
        args.append(nc.dram_tensor(f"in_{name}", array.shape, _mybir.dt.from_np(array.dtype),
                                   kind="ExternalInput").ap())
    args.append(nc.dram_tensor("out_y", (SEQ, D), _mybir.dt.float32, kind="ExternalOutput").ap())
    trunk(nc, *args)
    r = _run(nc, [feeds], core_ids=[0])
    return r.results[0]["out_y"].reshape(a["x"].shape)
```
